# Optimizing a Trainium2 kernel written in Bass

```python
import jax, jax.numpy as jnp
from jax import lax
import numpy as np

D_MODEL = 1024
BATCH = 1
SEQ = 512
DEPTH = 2
DEC_BATCH = 8
DEC_SEQ = 1
PAST_LEN = 1024
PAGE_SIZE = 128

HEAD_DIM = 64
ROT_DIM = HEAD_DIM // 4
ROPE_THETA = 500000.0
ATTN_SCALE = HEAD_DIM ** -0.5
A_HEADS = 12
A_KV_HEADS = 4
IDX_HEADS = 8
IDX_DIM = 64
IDX_SCALE = (IDX_HEADS * IDX_DIM) ** -0.5
TOPK_MAX = 256
B_GROUPS = ((128, 1), (512, 4), (2048, 16))
B_HEADS = 4
MEM_LEN = 256
MEM_HEADS = 4
D_FF = 2816
EPS = 1e-6
Q_BLOCK = 128
N_A = (DEPTH + 1) // 2
N_B = DEPTH // 2
A_IN = (A_HEADS + 2 * A_KV_HEADS + MEM_HEADS) * HEAD_DIM + IDX_HEADS * IDX_DIM + IDX_DIM + IDX_HEADS
A_OUT = (A_HEADS + MEM_HEADS) * HEAD_DIM
B_IN = (len(B_GROUPS) * 3 * B_HEADS + MEM_HEADS) * HEAD_DIM
B_OUT = (B_HEADS + MEM_HEADS) * HEAD_DIM

kernel_name = 'dsa_dilated_hybrid_decoder_step'

def rmsnorm(x, g):
    xf = x.astype(jnp.float32)
    y = xf * lax.rsqrt(jnp.mean(xf * xf, axis=-1, keepdims=True) + EPS)
    return (y * g.astype(jnp.float32)).astype(x.dtype)

def rope(x, pos):
    half = ROT_DIM // 2
    inv = jnp.power(ROPE_THETA, -jnp.arange(half, dtype=jnp.float32) / half)
    ang = pos.astype(jnp.float32)[:, None] * inv[None, :]
    shp = (pos.shape[0],) + (1,) * (x.ndim - 3) + (half,)
    cos, sin = jnp.cos(ang).reshape(shp), jnp.sin(ang).reshape(shp)
    xr = x[..., :ROT_DIM].astype(jnp.float32)
    x1, x2 = xr[..., :half], xr[..., half:]
    rot = jnp.concatenate([x1 * cos - x2 * sin, x2 * cos + x1 * sin], axis=-1).astype(x.dtype)
    return jnp.concatenate([rot, x[..., ROT_DIM:]], axis=-1)

def swiglu(x, w_in, w_out):
    g, u = jnp.split(x @ w_in, 2, axis=-1)
    return (jax.nn.silu(g) * u) @ w_out

def memory_kv(mem, g, w):
    b = mem.shape[0]
    return (rmsnorm(mem, g) @ w).reshape(b, MEM_LEN, 2, MEM_HEADS, HEAD_DIM)

def mem_attention(q, mem_kv):
    s = jnp.einsum('bthd,bmhd->bhtm', q, mem_kv[:, :, 0]).astype(jnp.float32) * ATTN_SCALE
    p = jax.nn.softmax(s, axis=-1).astype(mem_kv.dtype)
    o = jnp.einsum('bhtm,bmhd->bthd', p, mem_kv[:, :, 1])
    return o.reshape(q.shape[0], q.shape[1], MEM_HEADS * HEAD_DIM)

def prep_a(p, pos):
    b, t = p.shape[:2]
    sizes = (A_HEADS * HEAD_DIM, A_KV_HEADS * HEAD_DIM, A_KV_HEADS * HEAD_DIM,
             IDX_HEADS * IDX_DIM, IDX_DIM, IDX_HEADS)
    q, k, v, iq, ik, iw, mq = jnp.split(p, np.cumsum(sizes).tolist(), axis=-1)
    q = rope(q.reshape(b, t, A_HEADS, HEAD_DIM), pos)
    k = rope(k.reshape(b, t, A_KV_HEADS, HEAD_DIM), pos)
    v = v.reshape(b, t, A_KV_HEADS, HEAD_DIM)
    iq = rope(iq.reshape(b, t, IDX_HEADS, IDX_DIM), pos)
    ik = rope(ik[:, :, None, :], pos)[:, :, 0, :]
    iw = iw.astype(jnp.float32) * IDX_SCALE
    kv = jnp.stack([k, v], axis=2)
    return q, kv, iq, ik, iw, mq.reshape(b, t, MEM_HEADS, HEAD_DIM)

def indexer_scores(iq, ik, iw, qpos, kpos):
    rel = jax.nn.relu(jnp.einsum('bthd,bsd->bths', iq, ik).astype(jnp.float32))
    sc = jnp.einsum('bths,bth->bts', rel, iw)
    return jnp.where(kpos[None, None, :] <= qpos[None, :, None], sc, -jnp.inf)

def gqa_sparse_attend(q, kv_sel, valid):
    b, t, h, dh = q.shape
    qg = q.reshape(b, t, A_KV_HEADS, h // A_KV_HEADS, dh)
    s = jnp.einsum('btngd,btknd->btngk', qg, kv_sel[:, :, :, 0]).astype(jnp.float32) * ATTN_SCALE
    s = jnp.where(valid[:, :, None, None, :], s, -jnp.inf)
    pr = jax.nn.softmax(s, axis=-1).astype(kv_sel.dtype)
    o = jnp.einsum('btngk,btknd->btngd', pr, kv_sel[:, :, :, 1])
    return o.reshape(b, t, h * dh)

def mixer_a_prompt(p):
    b, s = p.shape[:2]
    pos = jnp.arange(s)
    q, kv, iq, ik, iw, mq = prep_a(p, pos)
    n_sel = min(TOPK_MAX, s // 4)
    take = jax.vmap(lambda a, ix: a[ix])

    def block(t0):
        sl = lambda a: lax.dynamic_slice_in_dim(a, t0, Q_BLOCK, axis=1)
        sc = indexer_scores(sl(iq), ik, sl(iw), t0 + jnp.arange(Q_BLOCK), pos)
        vals, idx = lax.top_k(sc, n_sel)
        return gqa_sparse_attend(sl(q), take(kv, idx), jnp.isfinite(vals))

    o = lax.map(block, jnp.arange(s // Q_BLOCK) * Q_BLOCK)
    o = jnp.moveaxis(o, 0, 1).reshape(b, s, A_HEADS * HEAD_DIM)
    return o, mq, kv, ik

def mixer_a_sample(p, kv_pool, kidx_pool, page_table):
    b, t = p.shape[:2]
    pos = PAST_LEN + jnp.arange(t)
    q, kv, iq, ik, iw, mq = prep_a(p, pos)
    n_len = PAST_LEN + t
    n_sel = min(TOPK_MAX, n_len // 4)
    ik_past = kidx_pool[page_table].reshape(b, PAST_LEN, IDX_DIM)
    ik_all = jnp.concatenate([ik_past, ik], axis=1)
    sc = indexer_scores(iq, ik_all, iw, pos, jnp.arange(n_len))
    vals, idx = lax.top_k(sc, n_sel)
    ip = jnp.minimum(idx, PAST_LEN - 1)
    phys = jax.vmap(lambda pt, lp: pt[lp])(page_table, ip // PAGE_SIZE)
    rows = phys * PAGE_SIZE + ip % PAGE_SIZE
    kv_past = kv_pool.reshape((-1,) + kv_pool.shape[2:])[rows]
    kv_new = jax.vmap(lambda a, ix: a[ix])(kv, jnp.clip(idx - PAST_LEN, 0, t - 1))
    kv_sel = jnp.where((idx < PAST_LEN)[..., None, None, None], kv_past, kv_new)
    o = gqa_sparse_attend(q, kv_sel, jnp.isfinite(vals))
    return o, mq, kv, ik

def prep_b(p, pos):
    b, t = p.shape[:2]
    nqkv = len(B_GROUPS) * 3 * B_HEADS * HEAD_DIM
    qkv = p[..., :nqkv].reshape(b, t, len(B_GROUPS), 3, B_HEADS, HEAD_DIM)
    mq = p[..., nqkv:].reshape(b, t, MEM_HEADS, HEAD_DIM)
    q = rope(qkv[:, :, :, 0], pos)
    kv = jnp.stack([rope(qkv[:, :, :, 1], pos), qkv[:, :, :, 2]], axis=3)
    return q, kv, mq

def dilated_offsets(base, n_q, window, dil):
    return base + np.arange(n_q)[:, None] - dil * np.arange(window // dil + 1)[None, :]

def dilated_stats(q, sel, valid):
    s = jnp.einsum('bthd,btnhd->bthn', q, sel[:, :, :, 0]).astype(jnp.float32) * ATTN_SCALE
    s = jnp.where(valid[:, None, :], s, -jnp.inf)
    m = jnp.max(s, axis=-1, keepdims=True)
    e = jnp.exp(s - m)
    den = jnp.sum(e, axis=-1)
    o = jnp.einsum('bthn,btnhd->bthd', e, sel[:, :, :, 1].astype(jnp.float32)) / den[..., None]
    return o, m[..., 0], den

def combine_groups(stats):
    o = jnp.stack([st[0] for st in stats])
    m = jnp.stack([st[1] for st in stats])
    den = jnp.stack([st[2] for st in stats])
    wgt = den * jnp.exp(m - jnp.max(m, axis=0, keepdims=True))
    return jnp.sum(wgt[..., None] * o, axis=0) / jnp.sum(wgt, axis=0)[..., None]

def mixer_b_prompt(p):
    b, s = p.shape[:2]
    q, kv, mq = prep_b(p, jnp.arange(s))
    kv_pad = [jnp.pad(kv[:, :, g], ((0, 0), (w, 0), (0, 0), (0, 0), (0, 0)))
              for g, (w, d) in enumerate(B_GROUPS)]

    def block(t0):
        qb = lax.dynamic_slice_in_dim(q, t0, Q_BLOCK, axis=1)
        stats = []
        for g, (w, d) in enumerate(B_GROUPS):
            win = lax.dynamic_slice_in_dim(kv_pad[g], t0, w + Q_BLOCK, axis=1)
            loc = dilated_offsets(w, Q_BLOCK, w, d)
            stats.append(dilated_stats(qb[:, :, g], win[:, loc], (t0 - w + loc) >= 0))
        return combine_groups(stats)

    o = lax.map(block, jnp.arange(s // Q_BLOCK) * Q_BLOCK)
    o = jnp.moveaxis(o, 0, 1).reshape(b, s, B_HEADS * HEAD_DIM).astype(p.dtype)
    bufs = [kv[:, s - min(w, s):, g] for g, (w, d) in enumerate(B_GROUPS)]
    return o, mq, bufs

def mixer_b_sample(p, bufs):
    b, t = p.shape[:2]
    q, kv, mq = prep_b(p, PAST_LEN + jnp.arange(t))
    stats, new_bufs = [], []
    for g, (w, d) in enumerate(B_GROUPS):
        cat = jnp.concatenate([bufs[g], kv[:, :, g]], axis=1)
        loc = dilated_offsets(bufs[g].shape[1], t, w, d)
        stats.append(dilated_stats(q[:, :, g], cat[:, np.maximum(loc, 0)], loc >= 0))
        new_bufs.append(cat[:, cat.shape[1] - min(w, PAST_LEN + t):])
    o = combine_groups(stats).reshape(b, t, B_HEADS * HEAD_DIM).astype(p.dtype)
    return o, mq, new_bufs

def setup_inputs(seed: int = 0) -> dict:
    key = jax.random.key(seed)
    ks = jax.random.split(key, 24)
    n_pages = PAST_LEN // PAGE_SIZE
    n_used = DEC_BATCH * n_pages
    n_pool = n_used + (n_used + 3) // 4
    nrm = lambda k, shape, sc=1.0: jax.random.normal(k, shape, jnp.float32) * sc
    x_prompt = nrm(ks[0], (BATCH, SEQ, D_MODEL))
    x_sample = nrm(ks[1], (DEC_BATCH, DEC_SEQ, D_MODEL))
    cache_kv_a = nrm(ks[2], (N_A, n_pool, PAGE_SIZE, 2, A_KV_HEADS, HEAD_DIM))
    cache_kidx_a = nrm(ks[3], (N_A, n_pool, PAGE_SIZE, IDX_DIM))
    state_kv_b1 = nrm(ks[4], (N_B, DEC_BATCH, min(B_GROUPS[0][0], PAST_LEN), 2, B_HEADS, HEAD_DIM))
    state_kv_b2 = nrm(ks[5], (N_B, DEC_BATCH, min(B_GROUPS[1][0], PAST_LEN), 2, B_HEADS, HEAD_DIM))
    state_kv_b3 = nrm(ks[6], (N_B, DEC_BATCH, min(B_GROUPS[2][0], PAST_LEN), 2, B_HEADS, HEAD_DIM))
    cache_mem_kv = nrm(ks[7], (DEPTH, DEC_BATCH, MEM_LEN, 2, MEM_HEADS, HEAD_DIM))
    page_table = jax.random.permutation(ks[8], n_pool)[:n_used].reshape(DEC_BATCH, n_pages).astype(jnp.int32)
    mem_prompt = nrm(ks[9], (BATCH, MEM_LEN, D_MODEL))
    ffn_norm = 1.0 + nrm(ks[10], (DEPTH, 2, D_MODEL), 0.02)
    w_ffn_in = nrm(ks[11], (DEPTH, 2, D_MODEL, 2 * D_FF), D_MODEL ** -0.5)
    w_ffn_out = nrm(ks[12], (DEPTH, 2, D_FF, D_MODEL), D_FF ** -0.5)
    mix_norm = 1.0 + nrm(ks[13], (DEPTH, D_MODEL), 0.02)
    mem_norm = 1.0 + nrm(ks[14], (DEPTH, D_MODEL), 0.02)
    w_mem_kv = nrm(ks[15], (DEPTH, D_MODEL, 2 * MEM_HEADS * HEAD_DIM), D_MODEL ** -0.5)
    w_in_a = nrm(ks[16], (N_A, D_MODEL, A_IN), D_MODEL ** -0.5)
    w_out_a = nrm(ks[17], (N_A, A_OUT, D_MODEL), A_OUT ** -0.5)
    w_in_b = nrm(ks[18], (N_B, D_MODEL, B_IN), D_MODEL ** -0.5)
    w_out_b = nrm(ks[19], (N_B, B_OUT, D_MODEL), B_OUT ** -0.5)
    final_norm = 1.0 + nrm(ks[20], (D_MODEL,), 0.02)
    return {'x_prompt': x_prompt, 'x_sample': x_sample, 'cache_kv_a': cache_kv_a,
            'cache_kidx_a': cache_kidx_a, 'state_kv_b1': state_kv_b1, 'state_kv_b2': state_kv_b2,
            'state_kv_b3': state_kv_b3, 'cache_mem_kv': cache_mem_kv, 'page_table': page_table,
            'mem_prompt': mem_prompt, 'ffn_norm': ffn_norm, 'w_ffn_in': w_ffn_in, 'w_ffn_out': w_ffn_out,
            'mix_norm': mix_norm, 'mem_norm': mem_norm, 'w_mem_kv': w_mem_kv, 'w_in_a': w_in_a,
            'w_out_a': w_out_a, 'w_in_b': w_in_b, 'w_out_b': w_out_b, 'final_norm': final_norm}

def reference(x_prompt, x_sample, cache_kv_a, cache_kidx_a, state_kv_b1, state_kv_b2, state_kv_b3,
              cache_mem_kv, page_table, mem_prompt, ffn_norm, w_ffn_in, w_ffn_out, mix_norm, mem_norm,
              w_mem_kv, w_in_a, w_out_a, w_in_b, w_out_b, final_norm):
    yp, ys = x_prompt, x_sample
    bufs_in = (state_kv_b1, state_kv_b2, state_kv_b3)
    kv_a_p, kidx_a_p, kv_a_s, kidx_a_s, mem_p = [], [], [], [], []
    b_p = ([], [], [])
    b_s = ([], [], [])
    for i in range(DEPTH):
        j = i // 2
        yp = yp + 0.5 * swiglu(rmsnorm(yp, ffn_norm[i, 0]), w_ffn_in[i, 0], w_ffn_out[i, 0])
        ys = ys + 0.5 * swiglu(rmsnorm(ys, ffn_norm[i, 0]), w_ffn_in[i, 0], w_ffn_out[i, 0])
        hp = rmsnorm(yp, mix_norm[i])
        hs = rmsnorm(ys, mix_norm[i])
        mkv_p = memory_kv(mem_prompt, mem_norm[i], w_mem_kv[i])
        mem_p.append(mkv_p)
        if i % 2 == 0:
            op, mqp, kvp, ikp = mixer_a_prompt(hp @ w_in_a[j])
            os_, mqs, kvs, iks = mixer_a_sample(hs @ w_in_a[j], cache_kv_a[j], cache_kidx_a[j], page_table)
            kv_a_p.append(kvp)
            kidx_a_p.append(ikp)
            kv_a_s.append(kvs)
            kidx_a_s.append(iks)
            w_out = w_out_a[j]
        else:
            op, mqp, bp = mixer_b_prompt(hp @ w_in_b[j])
            os_, mqs, bs = mixer_b_sample(hs @ w_in_b[j], [bf[j] for bf in bufs_in])
            for g in range(len(B_GROUPS)):
                b_p[g].append(bp[g])
                b_s[g].append(bs[g])
            w_out = w_out_b[j]
        yp = yp + jnp.concatenate([op, mem_attention(mqp, mkv_p).astype(op.dtype)], axis=-1) @ w_out
        ys = ys + jnp.concatenate([os_, mem_attention(mqs, cache_mem_kv[i]).astype(os_.dtype)], axis=-1) @ w_out
        yp = yp + 0.5 * swiglu(rmsnorm(yp, ffn_norm[i, 1]), w_ffn_in[i, 1], w_ffn_out[i, 1])
        ys = ys + 0.5 * swiglu(rmsnorm(ys, ffn_norm[i, 1]), w_ffn_in[i, 1], w_ffn_out[i, 1])
    y_prompt = rmsnorm(yp, final_norm)
    y_sample = rmsnorm(ys, final_norm)
    new_kv_a_prompt = jnp.stack(kv_a_p)
    new_kidx_a_prompt = jnp.stack(kidx_a_p)
    new_b1_prompt = jnp.stack(b_p[0])
    new_b2_prompt = jnp.stack(b_p[1])
    new_b3_prompt = jnp.stack(b_p[2])
    new_mem_kv_prompt = jnp.stack(mem_p)
    new_kv_a_sample = jnp.stack(kv_a_s)
    new_kidx_a_sample = jnp.stack(kidx_a_s)
    new_b1_sample = jnp.stack(b_s[0])
    new_b2_sample = jnp.stack(b_s[1])
    new_b3_sample = jnp.stack(b_s[2])
    return (y_prompt, y_sample, new_kv_a_prompt, new_kidx_a_prompt, new_b1_prompt, new_b2_prompt,
            new_b3_prompt, new_mem_kv_prompt, new_kv_a_sample, new_kidx_a_sample, new_b1_sample,
            new_b2_sample, new_b3_sample)


_drawn_inputs = setup_inputs


def setup_inputs(seed=0):
    import zlib

    import numpy as np

    out = dict(_drawn_inputs(seed))
    spreads = {}
    factors = {'ffn_norm': 2.732, 'mem_norm': 7.795, 'final_norm': 8.651}
    for name, (base, spread) in spreads.items():
        noise = np.random.default_rng([zlib.crc32(name.encode()), seed]).standard_normal(out[name].shape)
        drawn = base * np.exp(spread * noise) if base else spread * noise
        out[name] = __import__('jax').numpy.asarray(drawn.astype(out[name].dtype))
    for name, factor in factors.items():
        out[name] = (out[name] * factor).astype(out[name].dtype)
    return out
```

```python
from contextlib import ExitStack

import concourse.bass as bass
from concourse import mybir

F32 = mybir.dt.float32
F32R = mybir.dt.float32r
I32 = mybir.dt.int32
ALU = mybir.AluOpType
ACT = mybir.ActivationFunctionType
AX_X = mybir.AxisListType.X

P = 128
D = 1024
KT = D // P
SEQ, NSAMP = 512, 8
T = SEQ + NSAMP
TH = T // 2
NBLK = SEQ // P
FF = 2816
FT = FF // P
HALF_TILES = (12, FT - 12)
HD = 64
MEM = 256
PAST, PAGE = 1024, 128
NPAGE = PAST // PAGE
TOPK_PROMPT, TOPK_SAMPLE = 128, 256
SCALE = HD ** -0.5
IDX_SCALE = float((8 * 64) ** -0.5)
EPS = 1e-6
NEG = -1e30
TAKEN = -3e38
CH = 2048
NFFN = 4
FFN_CHUNKS = FT + 2 * KT

ROWS_A, ROWS_4 = NSAMP * 12, NSAMP * 4
PAIRS_A = [(0, 3), (1, 4), (2, 5), (6, 9), (7, 10), (8, 11)]
WINDOWS = [(128, 1), (512, 4), (2048, 16)]
KEYS_B = [128, 128, 64]
COLS_A = PAST + NSAMP
COLS_B = sum(KEYS_B) + 3 * NSAMP
SLOTS = 6
ITEMS = {"idx": (4, 2 * PAST, 0), "a": (1, 2 * PAST, 2 * PAST), "mem": (4, 2 * MEM, 2 * MEM), "b": (2, 640, 768)}


def chunk_plan():
    plan, n = {}, 0
    for name, count in (("mem", 4), ("ffn0", FFN_CHUNKS), ("in_a", 9), ("out_a", 4), ("ffn1", FFN_CHUNKS),
                        ("ffn2", FFN_CHUNKS), ("in_b", 10), ("out_b", 2), ("ffn3", FFN_CHUNKS)):
        plan[name] = n
        n += count
    return plan, n


def ring_plan():
    items, loads, last = [], [0] * SLOTS, [None] * SLOTS
    for what, kind, layer in (("key", "idx", 0), ("key", "mem", 0), ("value", "mem", 0), ("key", "a", 0),
                              ("value", "a", 0), ("key", "mem", 1), ("value", "mem", 1), ("key", "b", 1),
                              ("value", "b", 1)):
        per = ITEMS[kind][0]
        for first in range(0, NSAMP, per):
            r = len(items)
            slot = r if kind == "idx" else (r - 2) % SLOTS
            dmas = per * NPAGE if kind in ("idx", "a") else 1
            loads[slot] += 16 * dmas
            items.append(dict(what=what, kind=kind, layer=layer, first=first, r=r, slot=slot, loaded=loads[slot],
                              after=last[slot]))
            last[slot] = r
    return items


def units_a():
    units = units_mem(6)
    for blk in range(NBLK):
        for tile, pair in enumerate(PAIRS_A):
            for half in range(2):
                units.append(dict(kind="a", blk=blk, tile=tile, half=half, cols=(blk + 1) * P,
                                  kv=2 * (tile // 3) + half, out=tile))
    return units


def units_mem(first_out):
    return [dict(kind="mem", blk=blk, tile=tile, half=half, cols=MEM, kv=2 * tile + half, out=first_out + tile)
            for blk in range(NBLK) for tile in range(2) for half in range(2)]


def units_b():
    return [dict(kind="b", blk=r, tile=tile, half=half, cols=768, kv=2 * tile + half, out=tile)
            for r in range(4) for tile in range(2) for half in range(2)]


def build(nc, ins, outs):
    plan, n_chunks = chunk_plan()
    with ExitStack() as ctx:
        def sb(name, shape, dt=F32):
            return ctx.enter_context(nc.sbuf_tensor(name, shape, dt))

        def sem(name):
            return ctx.enter_context(nc.semaphore(name))

        arena_at = (nc.sbuf_base + 31) // 32 * 32
        arena = sb("arena", [P, (2 * KT + 24) * T + 4 * CH])

        def placed(name, shape, dt, at):
            return nc.alloc_sbuf_tensor_at(name, shape, dt, offset=arena_at + 4 * at)

        y = sb("y", [P, KT, T])
        X_AT, ACT_AT, W_AT = 0, 2 * KT * T, (2 * KT + 24) * T
        xh = placed("xh", [P, KT, T], F32R, X_AT)
        xl = placed("xl", [P, KT, T], F32R, X_AT + KT * T)
        acth = placed("acth", [P, 12, T], F32R, ACT_AT)
        actl = placed("actl", [P, 12, T], F32R, ACT_AT + 12 * T)
        raw = sb("raw", [P, 2, CH])
        wh = placed("wh", [P, 2, CH], F32R, W_AT)
        wl = placed("wl", [P, 2, CH], F32R, W_AT + 2 * CH)
        tg = sb("tg", [P, 2, T])
        tu = sb("tu", [P, 2, T])
        rstd = sb("rstd", [P, T])
        ssum = sb("ssum", [P, T])
        qmem = ssum[:, 0:2 * ROWS_4 * NSAMP]
        rtok = sb("rtok", [P, 9])
        memk = sb("memk", [P, 2, 2, MEM])
        memv = sb("memv", [P, 2, 2, MEM])
        gains = sb("gains", [P, 9, KT])
        cosf = sb("cosf", [P, T])
        sinf = sb("sinf", [P, T])
        rot = sb("rot", [P, P])
        ident = sb("ident", [P, P])
        ones = sb("ones", [P, P])
        causal = sb("causal", [P, P])
        small = sb("small", [P, 64 + 64 + 96 + 8 + 32])
        stats = sb("stats", [P, 4, 4])
        rstat = sb("rstat", [P, 4])
        tk = sb("tk", [P, 4, 10])
        iwt = sb("iwt", [P, NBLK, 8])
        iws = sb("iws", [64, 8])
        scs = sb("scs", [P, COLS_A])
        work = sb("work", [P, COLS_A])
        tkw = sb("tkw", [P, 768])
        qblk = sb("qblk", [P, 2 * ROWS_A * NSAMP])
        ring = sb("ring", [P, 2, CH])
        ring_w = placed("ring_w", [P, 4, CH], F32, W_AT)
        pages = sb("pages", [1, NSAMP * NPAGE], I32)
        epsb = sb("epsb", [P, 1])

        e8, selm, e96, offm, offb = (small[0:8, 0:64], small[0:64, 64:72], small[0:8, 128:224],
                                     small[0:8, 224:232], small[0:32, 232:256])
        tiles = placed("tiles", [P, 16, T], F32, ACT_AT)
        VALUES_AT = ACT_AT + 16 * T
        a_tiles = [tiles[:, i, :] for i in range(16)]
        a_v = placed("a_v", [P, NBLK, 256], F32, VALUES_AT)
        a_vs = placed("a_vs", [8, 256], F32, VALUES_AT + 1024)
        a_maskb = placed("a_maskb", [P, 1152], F32, VALUES_AT + 1280)
        a_sc = placed("a_sc", [P, 1152], F32, VALUES_AT + 2432)
        b_tiles = a_tiles[:14]
        b_v = placed("b_v", [P, 3, NBLK, 256], F32, VALUES_AT)
        b_vs = placed("b_vs", [8, 3, 256], F32, VALUES_AT + 3072)
        b_mask = [scs[:, 0:768], tkw[:, 0:768]]
        pbuf = placed("pbuf", [P, 2048], F32, X_AT)
        ptb = placed("ptb", [P, 2, 512], F32, X_AT + 2048)
        diag = placed("diag", [P, 4, P], F32, X_AT + 3072)
        rowp = placed("rowp", [P, COLS_A], F32, X_AT)
        rowt = placed("rowt", [P, 9, ROWS_A], F32, X_AT + 1040)
        ot = placed("ot", [P, KT, T], F32, X_AT + KT * T)
        mraw = placed("mraw", [P, KT, MEM], F32, ACT_AT)
        mh = placed("mh", [P, KT, MEM], F32R, ACT_AT + 2048)
        ml = placed("ml", [P, KT, MEM], F32R, ACT_AT + 4096)
        msq = placed("msq", [P, KT, MEM], F32, ACT_AT + 6144)
        msum = placed("msum", [P, MEM], F32, ACT_AT + 8192)
        mrstd = placed("mrstd", [P, MEM], F32, ACT_AT + 8448)
        mrtok = placed("mrtok", [P, 2], F32, ACT_AT + 8704)

        ps = ctx.enter_context(nc.psum_tensor("ps", [P, 8, 512], F32))
        psf = ps[:, :, :].rearrange("p b c -> p (b c)")

        def halves(x):
            return x.rearrange("p (h t) -> p h t", h=2)

        def bank2(b):
            return ps[:, b:b + 2, 0:TH]

        const_loaded = sem("const_loaded"); rope_loaded = sem("rope_loaded"); y_loaded = sem("y_loaded"); mem_loaded = sem("mem_loaded")
        pages_loaded = sem("pages_loaded"); ones_set = sem("ones_set")
        w_loaded = [sem("w_loaded0"), sem("w_loaded1")]
        w_head = sem("w_head"); w_rest = sem("w_rest"); w_used = sem("w_used")
        x_head = sem("x_head"); x_rest = sem("x_rest"); sq_ready = sem("sq_ready"); ssum_done = sem("ssum_done")
        rms_ready = sem("rms_ready"); rms_read = sem("rms_read"); tok_read = sem("tok_read")
        rstd_ready = sem("rstd_ready"); rtok_ready = sem("rtok_ready")
        gate_ready = sem("gate_ready"); up_ready = sem("up_ready")
        silu_ready = sem("silu_ready"); hid_ready = sem("hid_ready")
        act_head = sem("act_head"); act_rest = sem("act_rest"); y_added = sem("y_added")
        m_head = sem("m_head"); m_rest = sem("m_rest"); m_sq = sem("m_sq"); m_sum = sem("m_sum")
        m_rms = sem("m_rms"); m_sqrt = sem("m_sqrt"); m_rstd = sem("m_rstd"); m_first = sem("m_first")
        mkv_done = sem("mkv_done")
        t_ready = sem("t_ready"); raw_ready = sem("raw_ready"); rot_ready = sem("rot_ready")
        sin_ready = sem("sin_ready"); cos_ready = sem("cos_ready"); roped = sem("roped")
        v_ready = sem("v_ready"); v_done = sem("v_done"); out_first = sem("out_first")
        iw_ready = sem("iw_ready"); iw_done = sem("iw_done")
        ix_ready = sem("ix_ready"); ix_relu = sem("ix_relu"); ix_added = sem("ix_added")
        chain_done = sem("chain_done"); mask_ready = sem("mask_ready")
        six_relu = sem("six_relu"); six_sum = sem("six_sum"); six_done = sem("six_done")
        q_zeroed = sem("q_zeroed"); q_placed = sem("q_placed")
        r_loaded = [sem(f"r_loaded{i}") for i in range(SLOTS)]
        r_used = sem("r_used")
        s_ready = sem("s_ready"); s_masked = sem("s_masked"); nmax_ready = sem("nmax_ready")
        exp_ready = sem("exp_ready"); den_ready = sem("den_ready"); p_ready = sem("p_ready")
        pt_ready = sem("pt_ready"); pt_copied = sem("pt_copied"); pv_done = sem("pv_done"); o_stored = sem("o_stored")
        row_ready = sem("row_ready"); row_max = sem("row_max"); row_exp = sem("row_exp"); row_norm = sem("row_norm")
        rowt_ready = sem("rowt_ready"); rowt_copied = sem("rowt_copied"); rowo_stored = sem("rowo_stored")
        ot_head = sem("ot_head"); ot_rest = sem("ot_rest")
        bmask_loaded = [sem("bmask_loaded0"), sem("bmask_loaded1")]
        out_written = sem("out_written"); fin_ready = sem("fin_ready"); copied = sem("copied")

        units = [units_a(), units_mem(2) + units_b()]
        items = ring_plan()

        def place(all_units):
            group = 0
            for u, q in enumerate(all_units):
                wide = q["kind"] == "b"
                q.update(u=u, pair=u // 2, s0=(u % 2) * 1024 if wide else (u % 4) * 512, groups=[],
                         size=1024 if wide else 512)
                for at in range(0, q["cols"] // P, 3 if wide else 4):
                    q["groups"].append((group, at, min(3 if wide else 4, q["cols"] // P - at)))
                    group += 1
                q["before"] = next((v for v in reversed(all_units[:u])
                                    if v["s0"] < q["s0"] + q["size"] and q["s0"] < v["s0"] + v["size"]), None)

        place(units[0] + units[1])
        SC0 = {1: 0, 2: 256, 3: 640}
        V_AT = {0: 0, 1: 5}
        A_ROPED = [i for i in range(16) if i not in (5, 14, 15)]
        mixers = [
            dict(layer=0, norm=1, chunk=plan["in_a"], out_chunk=plan["out_a"], ntiles=16, tile0=0, rope0=0,
                 roped=A_ROPED, tiles=a_tiles, v0=0, v_units=[(0, tb) for tb in range(5)], acc=16, out_kt=8, ot0=0,
                 out0=0, mem_q=14),
            dict(layer=1, norm=4, chunk=plan["in_b"], out_chunk=plan["out_b"], ntiles=14, tile0=16, rope0=13,
                 roped=list(range(12)), tiles=b_tiles, v0=5, v_units=[(g, tb) for g in range(3) for tb in range(5)],
                 acc=56, out_kt=4, ot0=8, out0=4, mem_q=12)]
        FFN_ACC = [0, 24, 40, 64]
        FFN_NORM = [0, 2, 3, 5]
        ROW_KIND = ["mem", "a", "mem", "b"]
        ROW_LAYER = [0, 0, 1, 1]
        SEARCH_STEPS = 3 * (TOPK_PROMPT // 8 + 1) + TOPK_SAMPLE // 8 + 1
        Q_PLACED = {"idx": 16, 0: 20, 1: 32, 2: 36, 3: 48}
        Q_ZEROED = {"idx": 1, 0: 2, 1: 3, 2: 4, 3: 5}

        def slot(i):
            return ring[:, i, :] if i < 2 else ring_w[:, i - 2, :]

        def nrows(kind):
            return ROWS_A if kind == "a" else ROWS_4

        def row_tiles(kind):
            if kind == "a":
                return [(i * P, P) for i in range(NPAGE)] + [(PAST, NSAMP)]
            if kind == "b":
                return [(0, 128), (128, 128), (256, 64)] + [(320 + NSAMP * g, NSAMP) for g in range(3)]
            return [(0, 128), (128, 128)]

        def row_cols(kind):
            return {"a": COLS_A, "b": COLS_B, "mem": MEM}[kind]

        def tokens(tb, g):
            if tb == 4:
                return slice(SEQ, T)
            return slice(tb * P, (tb + 1) * P) if g == 0 else slice(tb, SEQ, 4)

        def rtok_col(tb, g):
            return tb if g == 0 or tb == 4 else 5 + tb

        def tile_done(M, t):
            if t % 2:
                return w_used, M["chunk"] + t // 2 + 1
            return t_ready, (M["tile0"] + t) // 2 + 1

        def v_block_done(M, i):
            if M["v_units"][i][1] == 4:
                return w_used, M["chunk"] + M["ntiles"] // 2 + i // 5 + 1
            return v_ready, 4 * ((M["v0"] + i) // 5) + i % 5 + 1

        def out_tiles_per_chunk(M):
            return CH // (M["out_kt"] * P)

        def out_done(M, m):
            per = out_tiles_per_chunk(M)
            if m % per == per - 1:
                return w_used, M["out_chunk"] + m // per + 1
            return out_first, (0 if M["layer"] == 0 else 4) + m - m // per + 1

        a_items = [it["r"] for it in items if it["kind"] == "a"]
        BY_SCALAR = a_items[7::2]

        def page_number(eng, at, src):
            return eng.value_load(pages[0:1, at:at + 1], min_val=0, max_val=ins[src].shape[0] - 1)

        def load_pages(eng, it):
            src = "kpool" if it["what"] == "key" else "vpool"
            numbers = [page_number(eng, it["first"] * NPAGE + k, src) for k in range(NPAGE)]
            for k, page in enumerate(numbers):
                eng.dma_start(slot(it["slot"])[:, k * 256:(k + 1) * 256],
                              ins[src][bass.ds(page, 1)].rearrange("a p c -> (a p) c")).then_inc(r_loaded[it["slot"]], 16)

        block = ctx.enter_context(nc.Block())

        @block.sync
        def _(sp):
            sp.dma_start(mraw[:, :, :], ins["mem_x"]).then_inc(mem_loaded, 16)
            for t, src in ((gains[:, :, :], "gains"), (ident[:, :], "ident"), (small[:, :], "small"),
                           (epsb[:, :], "eps")):
                sp.dma_start(t, ins[src]).then_inc(const_loaded, 16)
            sp.dma_start(raw[:, 0, :], ins["w_mem"][0]).then_inc(w_loaded[0], 16)
            sp.dma_start(raw[:, 1, :], ins["w_mem"][1]).then_inc(w_loaded[1], 16)
            sp.dma_start(y[:, :, :], ins["x"]).then_inc(y_loaded, 16)
            for t, src in ((cosf, "cos"), (sinf, "sin"), (rot, "rot"), (causal, "causal")):
                sp.dma_start(t[:, :], ins[src]).then_inc(rope_loaded, 16)
            sp.dma_start(pages[:, :], ins["pages"]).then_inc(pages_loaded, 16)

            def load(n, src):
                sp.wait_ge(w_head, n - 1)
                sp.wait_ge(w_rest, n - 1)
                sp.dma_start(raw[:, n % 2, 0:src.shape[1]], src).then_inc(w_loaded[n % 2], 16)

            def load_loop(n0, src, first, count, cols):
                with sp.Fori(0, count // 2) as i:
                    for b in range(2):
                        sp.wait_ge(w_head, 2 * i + (n0 + b - 1))
                        sp.wait_ge(w_rest, 2 * i + (n0 + b - 1))
                        sp.dma_start(raw[:, (n0 + b) % 2, 0:cols],
                                     src[bass.ds(2 * i + (first + b), 1)].rearrange("a p c -> (a p) c"))\
                            .then_inc(w_loaded[(n0 + b) % 2], 16)

            def ffn_loads(f):
                n = plan[f"ffn{f}"]
                for h in range(2):
                    count = HALF_TILES[h]
                    load_loop(n, ins["w_ffn_in"], f * FT + h * HALF_TILES[0], count, CH)
                    if f == 0:
                        for m in range(KT):
                            load(n + count + m, ins[f"w_ffn_out{h}"][m])
                            index_pages(h * KT + m)
                    else:
                        load_loop(n + count, ins[f"w_ffn_out{h}"], f * KT, KT, count * P)
                    n += count + KT

            def ring_loads(kind, what, layer):
                for it in items:
                    if (it["kind"], it["what"], it["layer"]) != (kind, what, layer) or it["r"] in BY_SCALAR:
                        continue
                    if it["after"] is not None:
                        sp.wait_ge(r_used, it["after"] + 1)
                    if it["slot"] >= 2:
                        sp.wait_ge(w_used, mixers[layer]["out_chunk"])
                    if kind == "a":
                        load_pages(sp, it)
                    else:
                        src = ins[f"{kind}_{what}"] if kind == "b" else ins[f"mem_{what}"][layer]
                        sp.dma_start(slot(it["slot"])[:, 0:src.shape[2]], src[it["first"] // ITEMS[kind][0]])\
                            .then_inc(r_loaded[it["slot"]], 16)

            def index_pages(part):
                b, k0 = part // 2, part % 2 * (NPAGE // 2)
                numbers = [page_number(sp, b * NPAGE + k0 + k, "kidx") for k in range(NPAGE // 2)]
                for k, page in enumerate(numbers):
                    at = (b % 4 // 2 * NPAGE + k0 + k) * P
                    sp.dma_start(ring[64 * (b % 2):64 * (b % 2) + 64, b // 4, at:at + P],
                                 ins["kidx"][bass.ds(page, 1)].rearrange("a p c -> (a p) c")).then_inc(r_loaded[b // 4], 16)

            load(2, ins["w_mem"][2])
            load(3, ins["w_mem"][3])
            sp.wait_ge(pages_loaded, 16)
            ffn_loads(0)
            for i in range(9):
                load(plan["in_a"] + i, ins["w_in_a"][i])
            for i in range(2):
                load(plan["out_a"] + i, ins["w_out_a"][i])
            for kind in ("mem", "a"):
                for what in ("key", "value"):
                    ring_loads(kind, what, 0)
            load(plan["out_a"] + 2, ins["w_out_a"][2])
            load(plan["out_a"] + 3, ins["w_out_a"][3])
            ffn_loads(1)
            ffn_loads(2)
            for i in range(10):
                load(plan["in_b"] + i, ins["w_in_b"][i])
            for i in range(2):
                load(plan["out_b"] + i, ins["w_out_b"][i])
            for r in range(2):
                sp.dma_start(b_mask[r], ins["mask_b"][r]).then_inc(bmask_loaded[r], 16)
            ring_loads("mem", "key", 1)
            ring_loads("mem", "value", 1)
            first_b = units[1][16]["u"]
            for r in range(2, 4):
                sp.wait_ge(s_masked, first_b + 4 * (r - 1))
                sp.dma_start(b_mask[r % 2], ins["mask_b"][r]).then_inc(bmask_loaded[r % 2], 16)
            ring_loads("b", "key", 1)
            ring_loads("b", "value", 1)
            ffn_loads(3)
            for m in range(KT):
                sp.wait_ge(fin_ready, m + 1)
                sp.dma_start(outs["y"][:, m, :], y[:, m, :]).then_inc(out_written, 16)
            sp.wait_ge(out_written, 16 * (2 + 4 + 3 + KT))
            sp.wait_ge(copied, 16 * 3 * NSAMP)

        @block.tensor
        def _(pe):
            def chunk_ready(n):
                pe.wait_ge(w_head, n + 1)
                pe.wait_ge(w_rest, n + 1)

            def product(out, heads, rests, xheads, xrests, nk, before=None):
                for kt in range(nk):
                    if before is not None:
                        before(kt)
                    for i, (w, x) in enumerate(((heads, xheads), (heads, xrests), (rests, xheads))):
                        for o, moving in zip(out, x(kt)):
                            mm = pe.matmul(o, w(kt), moving, start=(kt == 0 and i == 0),
                                           stop=(kt == nk - 1 and i == 2))
                return mm

            def by_halves(buf):
                return lambda kt: [buf[:, kt, h * TH:(h + 1) * TH] for h in range(2)]

            def tile_of(buf, slot, t, width=2):
                return lambda kt: buf[:, slot, (kt * width + t) * P:(kt * width + t + 1) * P]

            def two_banks(b):
                return [ps[:, b + h, 0:TH] for h in range(2)]

            def rms(norm, bank, tok_bank=None):
                pe.wait_ge(ssum_done, KT * (norm + 1))
                for h in range(2):
                    mm = pe.matmul(ps[:, bank + h, 0:TH], ones[:, :], ssum[:, h * TH:(h + 1) * TH], start=True, stop=True)
                if tok_bank is not None:
                    for g in range(2):
                        for tb in range(5 - g):
                            cols, c = tokens(tb, g), rtok_col(tb, g)
                            mm = pe.matmul(ps[0:(NSAMP if tb == 4 else P), tok_bank, c:c + 1], ssum[:, cols],
                                           ones[:, 0:1], start=True, stop=True)
                mm.then_inc(rms_ready, 1)

            def memory_keys_values():
                pe.wait_ge(ones_set, 1)
                pe.wait_ge(m_sum, 1)
                pe.matmul(ps[:, 6, 0:MEM], ones[:, :], msum[:, :], start=True, stop=True)
                for tb in range(2):
                    mm = pe.matmul(ps[:, 7, tb:tb + 1], msum[:, tb * P:(tb + 1) * P], ones[:, 0:1], start=True, stop=True)
                mm.then_inc(m_rms, 1)
                for layer in range(2):
                    def m_ready(kt, layer=layer):
                        pe.wait_ge(m_head, KT * layer + kt + 1)
                        pe.wait_ge(m_rest, KT * layer + kt + 1)
                    for part in range(2):
                        n = 2 * layer + part
                        chunk_ready(n)
                        for t in range(2):
                            unit = 2 * n + t
                            if unit >= 4:
                                pe.wait_ge(mkv_done, unit - 3)
                            if part == 0:
                                mm = product([ps[:, unit % 4, 0:MEM]], tile_of(wh, n % 2, t), tile_of(wl, n % 2, t),
                                             lambda kt: [mh[:, kt, :]], lambda kt: [ml[:, kt, :]], KT,
                                             m_ready if t == 0 else None)
                            else:
                                mm = product([ps[:, unit % 4, 0:MEM]], lambda kt: mh[:, kt, t * P:(t + 1) * P],
                                             lambda kt: ml[:, kt, t * P:(t + 1) * P],
                                             lambda kt: [wh[:, n % 2, kt * 256:(kt + 1) * 256]],
                                             lambda kt: [wl[:, n % 2, kt * 256:(kt + 1) * 256]], KT)
                            mm.then_inc(w_used if t else m_first, 1)
                pe.wait_ge(mkv_done, 8)
                pe.wait_ge(m_sqrt, 2)

            def ffn(f):
                n, g, acc, norm = plan[f"ffn{f}"], FT * f, FFN_ACC[f], FFN_NORM[f]
                for h in range(2):
                    count = HALF_TILES[h]

                    def in_chunk(n_, slot, s, gates=None):
                        chunk_ready(n_)
                        for t in range(2):
                            mm = product(two_banks(4 * s + 2 * t), tile_of(wh, slot, t), tile_of(wl, slot, t),
                                         by_halves(xh), by_halves(xl), KT, gates if t == 0 else None)
                            if t == 0 and gates is not None:
                                if acc:
                                    pe.wait_ge(y_added, acc)
                                rms(norm, 4)
                        mm.then_inc(w_used, 1)

                    def x_ready(kt):
                        pe.wait_ge(x_head, KT * norm + kt + 1)
                        pe.wait_ge(x_rest, KT * norm + kt + 1)

                    if h == 0:
                        if acc:
                            pe.wait_ge(y_added, acc - 1)
                        in_chunk(n, n % 2, 0, x_ready)
                        pe.wait_ge(rms_read, norm + 1)
                        in_chunk(n + 1, (n + 1) % 2, 1)
                    else:
                        pe.wait_ge(y_added, acc)
                    with pe.Fori(1 - h, count // 2) as i:
                        for b in range(2):
                            pe.wait_ge(up_ready, 2 * i + (g + b - 1))
                            in_chunk(2 * i + (n + b), (n + b) % 2, b)
                    n += count
                    g += count

                    def out_chunk(n_, slot, b, gates=None):
                        chunk_ready(n_)
                        product(two_banks(4 * b), tile_of(wh, slot, 0, 1), tile_of(wl, slot, 0, 1), by_halves(acth),
                                by_halves(actl), count, gates).then_inc(w_used, 1)

                    def hidden_ready(kt):
                        pe.wait_ge(act_head, g - count + kt + 1)
                        pe.wait_ge(act_rest, g - count + kt + 1)

                    pe.wait_ge(up_ready, g - 1)
                    out_chunk(n, n % 2, 0, hidden_ready)
                    pe.wait_ge(up_ready, g)
                    out_chunk(n + 1, (n + 1) % 2, 1)
                    with pe.Fori(1, KT // 2) as i:
                        for b in range(2):
                            pe.wait_ge(y_added, 2 * i + (acc + b - 1))
                            out_chunk(2 * i + (n + b), (n + b) % 2, b)
                    n += KT
                    acc += KT

            def tiles_in(M, first, last):
                norm, T0 = M["norm"], M["tile0"]

                def x_ready(kt):
                    pe.wait_ge(x_head, KT * norm + kt + 1)
                    pe.wait_ge(x_rest, KT * norm + kt + 1)

                for t in range(first, last + 1):
                    if t < last:
                        n = M["chunk"] + t // 2
                        if t % 2 == 0:
                            chunk_ready(n)
                        if t == 0:
                            pe.wait_ge(y_added, M["acc"] - 1)
                        if t == 1:
                            pe.wait_ge(rms_read, norm + 1)
                        if t == 2:
                            pe.wait_ge(tok_read, (norm + 2) // 3)
                        if t >= 3:
                            pe.wait_ge(raw_ready, T0 + t - 2)
                        done, _ = tile_done(M, t)
                        product(two_banks(2 * (t % 3)), tile_of(wh, n % 2, t % 2), tile_of(wl, n % 2, t % 2),
                                by_halves(xh), by_halves(xl), KT, x_ready if t == 0 else None).then_inc(done, 1)
                        if t == 0:
                            pe.wait_ge(y_added, M["acc"])
                            rms(norm, 2, 4)
                    if t > first and t - 1 in M["roped"]:
                        k = M["rope0"] + M["roped"].index(t - 1)
                        pe.wait_ge(raw_ready, T0 + t)
                        if k >= 1:
                            pe.wait_ge(sin_ready, k)
                        for h in range(2):
                            mm = pe.matmul(ps[:, 6 + h, 0:TH], rot[:, :], M["tiles"][t - 1][:, h * TH:(h + 1) * TH],
                                           start=True, stop=True)
                        mm.then_inc(rot_ready, 1)

            def ropes_before(M, t):
                return M["rope0"] + sum(i < t for i in M["roped"])

            def values_in(M):
                pe.wait_ge(raw_ready, M["tile0"] + M["ntiles"])
                for i, (g, tb) in enumerate(M["v_units"]):
                    n = M["chunk"] + M["ntiles"] // 2 + g
                    if tb == 0:
                        chunk_ready(n)
                    if i >= 3:
                        pe.wait_ge(v_done, M["v0"] + i - 2)
                    rows = NSAMP if tb == 4 else P
                    done, _ = v_block_done(M, i)
                    product([ps[0:rows, 2 * (i % 3), 0:256]], lambda kt: xh[:, kt, tokens(tb, g)],
                            lambda kt: xl[:, kt, tokens(tb, g)], lambda kt: [wh[:, n % 2, kt * 256:(kt + 1) * 256]],
                            lambda kt: [wl[:, n % 2, kt * 256:(kt + 1) * 256]], KT).then_inc(done, 1)
                pe.wait_ge(v_done, M["v0"] + len(M["v_units"]))
                pe.wait_ge(roped, ropes_before(M, M["ntiles"]))

            def scores(q, layer):
                if q["before"]:
                    pe.wait_ge(s_masked, q["before"]["u"] + 1)
                rows = slice(64 * q["half"], 64 * q["half"] + 64)
                if q["kind"] == "b":
                    for g in range(3):
                        every = slice(q["blk"], SEQ, 4)
                        keys = slice(0, SEQ) if g == 0 else every
                        at, w = q["s0"] + (0, SEQ, SEQ + P)[g], SEQ if g == 0 else P
                        mm = pe.matmul(psf[:, at:at + w], b_tiles[2 * g + q["tile"]][rows, every],
                                       b_tiles[6 + 2 * g + q["tile"]][rows, keys], start=True, stop=True)
                else:
                    if q["kind"] == "a":
                        queries, keys = a_tiles[6 + q["tile"]], a_tiles[12 + q["kv"] // 2][rows, 0:q["cols"]]
                    else:
                        queries, keys = a_tiles[mixers[layer]["mem_q"] + q["tile"]], memk[rows, layer, q["tile"], :]
                    mm = pe.matmul(psf[:, q["s0"]:q["s0"] + q["cols"]], queries[rows, q["blk"] * P:(q["blk"] + 1) * P],
                                   keys, start=True, stop=True)
                mm.then_inc(s_ready, 1)

            def turn(q):
                pe.wait_ge(p_ready, q["u"] + 1)
                for g, at, k in q["groups"]:
                    if g >= 2:
                        pe.wait_ge(pt_copied, g - 1)
                    for i in range(k):
                        mm = pe.matmul(ps[:, 4 + g % 2, i * P:(i + 1) * P],
                                       pbuf[:, q["s0"] + (at + i) * P:q["s0"] + (at + i + 1) * P],
                                       diag[:, q["u"] % 4, :], start=True, stop=True)
                    mm.then_inc(pt_ready, 1)

            def values_of(q, layer, tile):
                cols = slice(64 * q["kv"], 64 * q["kv"] + 64)
                if q["kind"] == "a":
                    return a_v[:, tile, cols]
                if q["kind"] == "b":
                    return b_v[:, 0, tile, cols] if tile < NBLK else b_v[:, tile - 3, q["blk"], cols]
                return memv[:, layer, tile, cols]

            def weigh(q, layer):
                if q["half"] == 0 and q["pair"] >= 2:
                    pe.wait_ge(o_stored, q["pair"] - 1)
                for g, at, k in q["groups"]:
                    pe.wait_ge(pt_copied, g + 1)
                    for i in range(k):
                        mm = pe.matmul(ps[64 * q["half"]:64 * q["half"] + 64, 6 + q["pair"] % 2, 0:P],
                                       values_of(q, layer, at + i), ptb[:, g % 2, i * P:(i + 1) * P],
                                       start=(at + i == 0), stop=(at + i == q["cols"] // P - 1))
                    mm.then_inc(pv_done, 1)

            def attend(layer, us):
                ahead = 2 if us[0]["kind"] == "b" else 3
                for q in us[:ahead]:
                    scores(q, layer)
                for k, q in enumerate(us):
                    if k + ahead < len(us):
                        scores(us[k + ahead], layer)
                    turn(q)
                    if k >= 1:
                        weigh(us[k - 1], layer)
                weigh(us[-1], layer)
                pe.wait_ge(o_stored, us[-1]["pair"] + 1)

            def indexer():
                pe.wait_ge(raw_ready, 6)
                pe.wait_ge(roped, 5)
                for tb in range(NBLK):
                    mm = pe.transpose(ps[:, 4, tb * 8:tb * 8 + 8], a_tiles[5][0:8, tb * P:(tb + 1) * P], ident[0:8, 0:8])
                mm = pe.matmul(ps[0:64, 5, 0:8], e8, a_tiles[5][0:8, SEQ:T], start=True, stop=True)
                mm.then_inc(iw_ready, 1)
                k = 0
                for blk in range(1, NBLK):
                    for h in range(8):
                        rows = slice(64 * (h % 2), 64 * (h % 2) + 64)
                        if k >= 4:
                            pe.wait_ge(ix_relu, k - 3)
                        pe.matmul(ps[:, k % 4, 0:(blk + 1) * P], a_tiles[h // 2][rows, blk * P:(blk + 1) * P],
                                  a_tiles[4][rows, 0:(blk + 1) * P], start=True, stop=True).then_inc(ix_ready, 1)
                        k += 1
                pe.wait_ge(ix_relu, k)
                pe.wait_ge(iw_done, 2)
                pe.wait_ge(q_placed, Q_PLACED["idx"])
                for pair in range(NSAMP // 2):
                    it = items[pair // 2]
                    pe.wait_ge(r_loaded[it["slot"]], it["loaded"])
                    stat, o = qmem[:, pair * 64:(pair + 1) * 64], pair % 2 * PAST
                    for j, keys in enumerate((slot(it["slot"])[:, o:o + 512], slot(it["slot"])[:, o + 512:o + PAST],
                                              a_tiles[4][:, SEQ:T])):
                        mm = pe.matmul(ps[0:64, j, 0:keys.shape[1]], stat, keys, start=(pair == 0), stop=(pair == 3))
                    if pair % 2:
                        mm.then_inc(r_used, 1)
                pe.wait_ge(six_relu, 1)
                for j, (at, w) in enumerate(((0, 512), (512, 512), (PAST, NSAMP))):
                    mm = pe.matmul(ps[0:8, 4 + j, 0:w], iws[:, :], work[0:64, at:at + w], start=True, stop=True)
                mm.then_inc(six_sum, 1)
                pe.wait_ge(six_done, 3)

            def rows_of(k):
                kind, layer = ROW_KIND[k], ROW_LAYER[k]
                rows, (per, kw, vw), nh = nrows(kind), ITEMS[kind], nrows(kind) // NSAMP
                pe.wait_ge(q_placed, Q_PLACED[k])
                q_at = qmem if kind == "mem" else qblk
                its = [it for it in items if it["kind"] == kind and it["layer"] == layer]
                for it in [it for it in its if it["what"] == "key"]:
                    pe.wait_ge(r_loaded[it["slot"]], it["loaded"])
                    for b in range(it["first"], it["first"] + per):
                        keys = slot(it["slot"])[:, (b - it["first"]) * kw:(b - it["first"] + 1) * kw]
                        for p in range(2):
                            one = b == 0 and p == 0
                            end = b == NSAMP - 1 and p == 1

                            def stat(g=0):
                                o = ((2 * g + p) * NSAMP + b) * rows
                                return q_at[:, o:o + rows]
                            if kind == "a":
                                paged = keys.rearrange("q (g p c) -> q g p c", g=NPAGE, p=2)
                                for j in range(2):
                                    pe.matmul(ps[0:rows, j, :], stat(), paged[:, 4 * j:4 * j + 4, p, :], start=one,
                                              stop=False)
                                mm = pe.matmul(ps[0:rows, 2, 0:NSAMP], stat(), a_tiles[12 + p][:, SEQ:T], start=one,
                                               stop=False)
                            elif kind == "mem":
                                mm = pe.matmul(ps[0:rows, 0, 0:MEM], stat(), keys[:, p * MEM:(p + 1) * MEM], start=one,
                                               stop=end)
                            else:
                                at = 0
                                for g, w in enumerate(KEYS_B):
                                    pe.matmul(ps[0:rows, 0, at:at + w], stat(g),
                                              keys[:, 2 * at + p * w:2 * at + (p + 1) * w], start=one and g == 0,
                                              stop=False, skip_group_check=True)
                                    at += w
                                for g in range(3):
                                    mm = pe.matmul(ps[0:rows, 0, 320 + NSAMP * g:328 + NSAMP * g], stat(g),
                                                   b_tiles[6 + 2 * g + p][:, SEQ:T], start=False, stop=False,
                                                   skip_group_check=True)
                    mm.then_inc(r_used, 1)
                if kind == "a":
                    pe.wait_ge(mask_ready, 4)
                    for j, (at, w) in enumerate(((0, 512), (512, 512), (PAST, NSAMP))):
                        mm = pe.matmul(ps[0:rows, j, 0:w], e96, scs[0:8, at:at + w], start=False, stop=True)
                    mm.then_inc(row_ready, 1)
                elif kind == "b":
                    pe.matmul(ps[0:rows, 0, 320:COLS_B], ident[0:rows, 0:rows], offb, start=False, stop=True,
                              skip_group_check=True).then_inc(row_ready, 1)
                pe.wait_ge(row_norm, k + 1)
                for i, (at, w) in enumerate(row_tiles(kind)):
                    mm = pe.transpose(ps[0:w, 4 + i // 5, (i % 5) * rows:(i % 5 + 1) * rows], rowp[0:rows, at:at + w],
                                      ident[0:rows, 0:rows])
                mm.then_inc(rowt_ready, 1)
                pe.wait_ge(rowt_copied, k + 1)
                for p in range(2):
                    if kind == "a":
                        pe.matmul(ps[:, 6 + p, 0:rows], a_vs[:, p * P:(p + 1) * P], rowt[0:NSAMP, 8, 0:rows],
                                  start=True, stop=False, skip_group_check=True)
                    elif kind == "b":
                        for g in range(3):
                            pe.matmul(ps[:, 6 + p, 0:rows], b_vs[:, g, p * P:(p + 1) * P], rowt[0:NSAMP, 3 + g, 0:rows],
                                      start=(g == 0), stop=False, skip_group_check=True)
                tiles_ = [i for i, (_, w) in enumerate(row_tiles(kind)) if w > NSAMP]
                for it in [it for it in its if it["what"] == "value"]:
                    pe.wait_ge(r_loaded[it["slot"]], it["loaded"])
                    for b in range(it["first"], it["first"] + per):
                        for p in range(2):
                            cols = slice(b * nh + p * nh // 2, b * nh + (p + 1) * nh // 2)
                            for i in tiles_:
                                w = row_tiles(kind)[i][1]
                                o = (b - it["first"]) * vw + i * 256 + p * P
                                mm = pe.matmul(ps[:, 6 + p, cols], slot(it["slot"])[0:w, o:o + P], rowt[0:w, i, cols],
                                               start=(kind == "mem" and b == 0 and i == 0), stop=(i == tiles_[-1]),
                                               skip_group_check=True)
                    mm.then_inc(r_used, 1)
                pe.wait_ge(rowo_stored, k + 1)

            def tiles_out(M):
                per, acc, nk = out_tiles_per_chunk(M), M["acc"], M["out_kt"]

                def o_ready(kt):
                    pe.wait_ge(ot_head, M["ot0"] + kt + 1)
                    pe.wait_ge(ot_rest, M["ot0"] + kt + 1)

                for m in range(KT):
                    n = M["out_chunk"] + m // per
                    if m % per == 0:
                        chunk_ready(n)
                    if m >= 2:
                        pe.wait_ge(y_added, acc + m - 1)
                    done, _ = out_done(M, m)
                    product(two_banks(4 * (m % 2)), tile_of(wh, n % 2, m % per, per), tile_of(wl, n % 2, m % per, per),
                            by_halves(acth), by_halves(actl), nk, o_ready if m == 0 else None).then_inc(done, 1)

            pe.wait_ge(const_loaded, 16 * 4)
            memory_keys_values()
            ffn(0)
            A, B = mixers
            pe.wait_ge(rope_loaded, 16 * 4)
            tiles_in(A, 0, 6)
            indexer()
            tiles_in(A, 6, 16)
            values_in(A)
            attend(0, units[0][:16])
            rows_of(0)
            attend(0, units[0][16:])
            rows_of(1)
            tiles_out(A)
            ffn(1)
            ffn(2)
            tiles_in(B, 0, 14)
            values_in(B)
            attend(1, units[1][:16])
            rows_of(2)
            attend(1, units[1][16:])
            rows_of(3)
            tiles_out(B)
            ffn(3)
            pe.wait_ge(y_added, 80)
            rms(6, 0)

        @block.scalar
        def _(act):
            def split(n, i=None):
                more = 0 if i is None else i
                act.wait_ge(w_loaded[n % 2], 16 * more + 16 * (n // 2 + 1))
                if n >= 2:
                    act.wait_ge(w_used, 2 * more + (n - 1))
                act.activation(wh[:, n % 2, :], raw[:, n % 2, :], ACT.Copy).then_inc(w_head, 1)

            copies = [0]

            def copy_state(count):
                for _ in range(count):
                    if copies[0] == 3 * NSAMP:
                        return
                    which, b = copies[0] % 3, copies[0] // 3
                    act.dma_start(outs[f"state{which}"][b], ins[f"state{which}"][b]).then_inc(copied, 16)
                    copies[0] += 1

            def prepare(norm, m, acc=None, i=None, last=False):
                at = m if i is None else 2 * i + m
                more = 0 if i is None else 2 * i
                if acc is not None:
                    act.wait_ge(y_added, more + (acc + m + 1))
                if norm > 0 or m >= 2:
                    act.wait_ge(ssum_done, more + (KT * norm + m - 1))
                tile = y[:, m, :] if i is None else y[:, bass.ds(at, 1), :].rearrange("p a t -> p (a t)")
                act.activation(tu[:, m % 2, :], tile, ACT.Square).then_inc(sq_ready, 1)
                if not last:
                    gain = gains[:, norm, m:m + 1] if i is None else gains[:, norm, bass.ds(at, 1)]
                    to = xh[:, m, :] if i is None else xh[:, bass.ds(at, 1), :].rearrange("p a t -> p (a t)")
                    act.activation(to, tile, ACT.Identity, scale=gain).then_inc(x_head, 1)

            def root(norm, bank, tok_bank=None):
                act.wait_ge(rms_ready, norm + 1)
                act.activation(halves(rstd[:, :]), bank2(bank), ACT.Sqrt, bias=epsb[:, 0:1], scale=1.0 / D)\
                   .then_inc(rms_read, 1)
                if tok_bank is not None:
                    for r, cols in ((P, slice(0, 4)), (NSAMP, slice(4, 5)), (P, slice(5, 9))):
                        a = act.activation(rtok[0:r, cols], ps[0:r, tok_bank, cols], ACT.Sqrt, bias=epsb[0:r, 0:1],
                                           scale=1.0 / D)
                    a.then_inc(tok_read, 1)

            def memory_keys_values():
                act.wait_ge(mem_loaded, 16)
                act.wait_ge(const_loaded, 64)
                act.activation(msq[:, :, :], mraw[:, :, :], ACT.Square).then_inc(m_sq, 1)
                for layer in range(2):
                    if layer:
                        act.wait_ge(w_used, 2)
                        act.wait_ge(m_rest, KT)
                    for kt in range(KT):
                        act.activation(mh[:, kt, :], mraw[:, kt, :], ACT.Identity,
                                       scale=gains[:, 7 + layer, kt:kt + 1]).then_inc(m_head, 1)
                    split(2 * layer)
                    split(2 * layer + 1)
                    if layer == 0:
                        act.wait_ge(m_rms, 1)
                        act.activation(mrstd[:, :], ps[:, 6, 0:MEM], ACT.Sqrt, bias=epsb[:, 0:1], scale=1.0 / D)\
                           .then_inc(m_sqrt, 1)
                        act.activation(mrtok[:, :], ps[:, 7, 0:2], ACT.Sqrt, bias=epsb[:, 0:1], scale=1.0 / D)\
                           .then_inc(m_sqrt, 1)
                split(4)
                split(5)
                act.wait_ge(y_loaded, 16)
                for m in range(KT):
                    prepare(0, m)
                act.wait_ge(mkv_done, 8)
                act.dma_start(outs["memk"], memk[:, :, :, :]).then_inc(out_written, 16)
                act.dma_start(outs["memv"], memv[:, :, :, :]).then_inc(out_written, 16)

            def ffn(f):
                n, g, acc, norm = plan[f"ffn{f}"], FT * f, FFN_ACC[f], FFN_NORM[f]
                for h in range(2):
                    count = HALF_TILES[h]

                    def in_tile(b, i):
                        act.wait_ge(gate_ready, 2 * i + (g + b + 1))
                        act.activation(tg[:, b, :], tg[:, b, :], ACT.Silu).then_inc(silu_ready, 1)
                        split(n + b + 2, i)
                        act.wait_ge(hid_ready, 2 * i + (g + b + 1))
                        act.activation(acth[:, bass.ds(2 * i + b, 1), :].rearrange("p a t -> p (a t)"), tg[:, b, :],
                                       ACT.Copy).then_inc(act_head, 1)
                    if h == 0:
                        root(norm, 4)
                    copy_state(2)
                    with act.Fori(0, count // 2) as i:
                        for b in range(2):
                            in_tile(b, i)
                    n += count
                    g += count
                    copy_state(2)
                    if h == 0:
                        with act.Fori(0, KT // 2) as i:
                            for b in range(2):
                                split(n + b + 2, i)
                    elif f < 3:
                        with act.Fori(0, KT // 2) as i:
                            for b in range(2):
                                split(n + b + 2, i)
                                prepare(norm_after(f), b, acc, i)
                    else:
                        for m in range(KT):
                            if m < KT - 2:
                                split(n + m + 2)
                            prepare(6, m, acc, last=True)
                    n += KT
                    acc += KT

            def tiles_in(M, first, last):
                for t in range(first, last):
                    if t == 0:
                        root(M["norm"], 2, 4)
                    if t % 2 == 1 and M["chunk"] + t // 2 + 2 < M["out_chunk"]:
                        split(M["chunk"] + t // 2 + 2)

            def values_in(M):
                for i, (g, tb) in enumerate(M["v_units"]):
                    done, count = v_block_done(M, i)
                    act.wait_ge(done, count)
                    act.wait_ge(rtok_ready, (M["norm"] + 2) // 3)
                    rows, col = NSAMP if tb == 4 else P, rtok_col(tb, g)
                    to = (a_vs[:, :] if tb == 4 else a_v[:, tb, :]) if M["layer"] == 0 else \
                        (b_vs[:, g, :] if tb == 4 else b_v[:, g, tb, :])
                    act.activation(to, ps[0:rows, 2 * (i % 3), 0:256], ACT.Copy, scale=rtok[0:rows, col:col + 1])\
                       .then_inc(v_done, 1)
                    if tb == 4 and M["chunk"] + M["ntiles"] // 2 + g + 2 < M["out_chunk"]:
                        split(M["chunk"] + M["ntiles"] // 2 + g + 2)
                act.wait_ge(v_done, M["v0"] + len(M["v_units"]))
                act.wait_ge(roped, M["rope0"] + len(M["roped"]))
                if M["layer"] == 0:
                    stores = ((outs["kidx"], a_tiles[4][0:64, :]), (outs["k_a"], tiles[:, 12:14, :]),
                              (outs["v_a"], a_v[:, :, :]), (outs["vs_a"], a_vs[:, :]))
                else:
                    stores = ((outs["k_b"], tiles[:, 6:12, :]), (outs["v_b"], b_v[:, :, :, :]),
                              (outs["vs_b"], b_vs[:, :, :]))
                for to, src in stores:
                    act.dma_start(to, src).then_inc(out_written, 16)

            def exponent(q):
                act.wait_ge(nmax_ready, q["u"] + 1)
                p = pbuf[:, q["s0"]:q["s0"] + q["cols"]]
                act.activation(p, p, ACT.Exp, bias=stats[:, 1, q["u"] % 4:q["u"] % 4 + 1], scale=SCALE,
                               accum_out=stats[:, 2, q["u"] % 4:q["u"] % 4 + 1]).then_inc(exp_ready, 1)

            def copy_turned(q, all_units):
                for g, at, k in q["groups"]:
                    act.wait_ge(pt_ready, g + 1)
                    if g >= 2:
                        act.wait_ge(pv_done, g - 1)
                    act.activation(ptb[:, g % 2, 0:k * P], ps[:, 4 + g % 2, 0:k * P], ACT.Copy).then_inc(pt_copied, 1)

            def attend(us):
                exponent(us[0])
                for k, q in enumerate(us):
                    if k + 1 < len(us):
                        exponent(us[k + 1])
                    copy_turned(q, us)

            def indexer():
                act.wait_ge(iw_ready, 1)
                act.activation(iwt[:, :, :].rearrange("p a b -> p (a b)"), ps[:, 4, 0:32], ACT.Copy, scale=IDX_SCALE)\
                   .then_inc(iw_done, 1)
                k = 0
                for blk in range(1, NBLK):
                    for h in range(8):
                        act.wait_ge(ix_ready, k + 1)
                        if k >= 2:
                            act.wait_ge(ix_added, k - 1)
                        act.activation(tg[:, k % 2, 0:(blk + 1) * P], ps[:, k % 4, 0:(blk + 1) * P], ACT.Relu)\
                           .then_inc(ix_relu, 1)
                        k += 1
                act.wait_ge(r_used, 2)
                act.activation(work[0:64, :], psf[0:64, 0:COLS_A], ACT.Relu).then_inc(six_relu, 1)

            def pages_of(rs):
                for it in items:
                    if it["r"] in rs:
                        act.wait_ge(r_used, it["after"] + 1)
                        load_pages(act, it)

            def rows_of(k):
                kind = ROW_KIND[k]
                rows, cols = nrows(kind), row_cols(kind)
                if kind == "a":
                    pages_of(BY_SCALAR[:-1])
                act.wait_ge(row_max, k + 1)
                act.activation(rowp[0:rows, 0:cols], psf[0:rows, 0:cols], ACT.Exp, bias=rstat[0:rows, 1:2], scale=SCALE,
                               accum_out=rstat[0:rows, 2:3]).then_inc(row_exp, 1)
                act.wait_ge(rowt_ready, k + 1)
                n = len(row_tiles(kind))
                parts = [(i, i + 1) for i in range(n) if row_tiles(kind)[i][1] < P]
                whole = sum(w == P for _, w in row_tiles(kind))
                parts = [(0, min(whole, 5))] + ([(5, whole)] if whole > 5 else []) + parts
                for a, b in parts:
                    w = row_tiles(kind)[a][1]
                    last = act.activation(rowt[0:w, a:b, 0:rows],
                                          ps[0:w, 4 + a // 5, (a % 5) * rows:(a % 5 + b - a) * rows]
                                          .rearrange("p (i r) -> p i r", r=rows), ACT.Copy)
                last.then_inc(rowt_copied, 1)
                if kind == "a":
                    pages_of(BY_SCALAR[-1:])

            def tiles_out(M):
                if M["layer"] == 0:
                    act.wait_ge(out_written, 16 * (2 + 4))
                else:
                    act.wait_ge(out_written, 16 * (2 + 4 + 3))
                act.wait_ge(rowo_stored, 2 * M["layer"] + 2)
                split(M["out_chunk"])
                split(M["out_chunk"] + 1)
                for kt in range(M["out_kt"]):
                    act.activation(acth[:, kt, :], ot[:, kt, :], ACT.Copy).then_inc(ot_head, 1)
                for m in range(KT):
                    if (m + 1) % out_tiles_per_chunk(M) == 0:
                        split(M["out_chunk"] + m // out_tiles_per_chunk(M) + 2)
                    prepare(M["norm"] + 1, m, M["acc"])

            def norm_after(f):
                return [1, 3, 4, 6][f]

            memory_keys_values()
            ffn(0)
            A, B = mixers
            tiles_in(A, 0, 6)
            indexer()
            tiles_in(A, 6, 16)
            values_in(A)
            attend(units[0][:16])
            rows_of(0)
            attend(units[0][16:])
            rows_of(1)
            tiles_out(A)
            ffn(1)
            ffn(2)
            tiles_in(B, 0, 14)
            values_in(B)
            attend(units[1][:16])
            rows_of(2)
            attend(units[1][16:])
            rows_of(3)
            tiles_out(B)
            ffn(3)
            root(6, 0)

        @block.vector
        def _(dve):
            def split(n, i=None):
                more = 0 if i is None else 2 * i
                dve.wait_ge(w_head, more + (n + 1))
                dve.tensor_tensor(wl[:, n % 2, :], raw[:, n % 2, :], wh[:, n % 2, :].bitcast(F32), ALU.subtract)\
                   .then_inc(w_rest, 1)

            def prepare(norm, m, i=None):
                more = 0 if i is None else 2 * i
                dve.wait_ge(x_head, more + (KT * norm + m + 1))
                if i is None:
                    tile, gain, head, rest = y[:, m, :], gains[:, norm, m:m + 1], xh[:, m, :], xl[:, m, :]
                else:
                    at = bass.ds(2 * i + m, 1)
                    tile, head, rest = (v[:, at, :].rearrange("p a t -> p (a t)") for v in (y, xh, xl))
                    gain = gains[:, norm, at]
                dve.scalar_tensor_tensor(rest, tile, gain, head.bitcast(F32), ALU.mult, ALU.subtract)\
                   .then_inc(x_rest, 1)

            def invert(norm, tok=False):
                dve.wait_ge(rms_read, norm + 1)
                dve.reciprocal(rstd[:, :], rstd[:, :]).then_inc(rstd_ready, 1)
                if tok:
                    dve.wait_ge(tok_read, (norm + 2) // 3)
                    for r, cols in ((P, slice(0, 4)), (NSAMP, slice(4, 5)), (P, slice(5, 9))):
                        d = dve.reciprocal(rtok[0:r, cols], rtok[0:r, cols])
                    d.then_inc(rtok_ready, 1)

            def add_out(scale, m, acc, done, count, i=None):
                more = 0 if i is None else 2 * i
                dve.wait_ge(done, more + count)
                if acc + m > 0:
                    dve.wait_ge(y_added, more + (acc + m))
                tile = y[:, m, :] if i is None else y[:, bass.ds(2 * i + m, 1), :].rearrange("p a t -> p (a t)")
                dve.scalar_tensor_tensor(halves(tile), bank2(4 * (m % 2)), scale, halves(tile), ALU.mult, ALU.add)\
                   .then_inc(y_added, 1)

            def memory_keys_values():
                dve.memset(ones[:, :], 1.0).then_inc(ones_set, 1)
                dve.wait_ge(m_sq, 1)
                dve.tensor_reduce(msum[:, :], msq[:, :, :].rearrange("p k t -> p t k"), AX_X, ALU.add).then_inc(m_sum, 1)
                for layer in range(2):
                    for kt in range(KT):
                        dve.wait_ge(m_head, KT * layer + kt + 1)
                        dve.scalar_tensor_tensor(ml[:, kt, :], mraw[:, kt, :], gains[:, 7 + layer, kt:kt + 1],
                                                 mh[:, kt, :].bitcast(F32), ALU.mult, ALU.subtract).then_inc(m_rest, 1)
                    split(2 * layer)
                    split(2 * layer + 1)
                    if layer == 0:
                        dve.wait_ge(m_sqrt, 2)
                        dve.reciprocal(mrstd[:, :], mrstd[:, :]).then_inc(m_rstd, 1)
                        dve.reciprocal(mrtok[:, :], mrtok[:, :]).then_inc(m_rstd, 1)
                        dve.wait_ge(m_rstd, 2)
                    for unit in range(4 * layer, 4 * layer + 4):
                        part, t = unit // 2 % 2, unit % 2
                        dve.wait_ge(w_used if t else m_first, unit // 2 + 1)
                        bank = ps[:, unit % 4, 0:MEM]
                        if part == 0:
                            dve.tensor_tensor(memk[:, layer, t, :], bank, mrstd[:, :], ALU.mult).then_inc(mkv_done, 1)
                        else:
                            dve.tensor_scalar(memv[:, layer, t, :], bank, mrtok[:, t:t + 1], None, ALU.mult)\
                               .then_inc(mkv_done, 1)
                split(4)
                split(5)
                for m in range(KT):
                    prepare(0, m)

            def ffn(f):
                n, g, acc, norm = plan[f"ffn{f}"], FT * f, FFN_ACC[f], FFN_NORM[f]
                for h in range(2):
                    count = HALF_TILES[h]

                    def in_tile(b, i, first=False):
                        more = 2 * i
                        dve.wait_ge(w_used, more + (n + b + 1))
                        if not first:
                            dve.wait_ge(act_rest, more + (g + b - 1))
                            dve.wait_ge(hid_ready, more + (g + b - 1))
                        dve.tensor_tensor(halves(tg[:, b, :]), bank2(4 * b), halves(rstd[:, :]), ALU.mult)\
                           .then_inc(gate_ready, 1)
                        dve.tensor_tensor(halves(tu[:, b, :]), bank2(4 * b + 2), halves(rstd[:, :]), ALU.mult)\
                           .then_inc(up_ready, 1)
                        split(n + b + 2, i)
                        dve.wait_ge(silu_ready, more + (g + b + 1))
                        dve.wait_ge(up_ready, more + (g + b + 1))
                        dve.tensor_tensor(tg[:, b, :], tg[:, b, :], tu[:, b, :], ALU.mult).then_inc(hid_ready, 1)

                    start = 0
                    if h == 0:
                        invert(norm)
                        dve.wait_ge(rstd_ready, [1, 3, 4, 6][f])
                        for b in range(2):
                            in_tile(b, 0, first=(f == 0))
                        start = 1
                    with dve.Fori(start, count // 2) as i:
                        for b in range(2):
                            in_tile(b, i)
                    n += count
                    g += count
                    if h == 0 or f < 3:
                        def out_tile(b, i):
                            add_out(0.5, b, acc, w_used, n + b + 1, i)
                            split(n + b + 2, i)
                            if h == 1:
                                prepare([1, 3, 4][f], b, i)
                        if acc == 0:
                            out_tile(0, 0)
                            out_tile(1, 0)
                        with dve.Fori(1 if acc == 0 else 0, KT // 2) as i:
                            for b in range(2):
                                out_tile(b, i)
                    else:
                        for m in range(KT):
                            add_out(0.5, m, acc, w_used, n + m + 1)
                            if m < KT - 2:
                                split(n + m + 2)
                    n += KT
                    acc += KT

            def tiles_in(M, first, last):
                def rotated(t):
                    k = M["rope0"] + M["roped"].index(t)
                    dve.wait_ge(rot_ready, k + 1)
                    if k >= 2:
                        dve.wait_ge(roped, k - 1)
                    dve.tensor_tensor(halves(tg[:, k % 2, :]), bank2(6), halves(sinf[:, :]), ALU.mult)\
                       .then_inc(sin_ready, 1)

                for t in range(first, last + 1):
                    if t == 0:
                        invert(M["norm"], True)
                        dve.wait_ge(rstd_ready, M["norm"] + 1)
                    if t < last:
                        done, count = tile_done(M, t)
                        dve.wait_ge(done, count)
                        dve.tensor_tensor(halves(M["tiles"][t]), bank2(2 * (t % 3)), halves(rstd[:, :]), ALU.mult)\
                           .then_inc(raw_ready, 1)
                        if t % 2 == 1 and M["chunk"] + t // 2 + 2 < M["out_chunk"]:
                            split(M["chunk"] + t // 2 + 2)
                    if t > first and t - 1 in M["roped"]:
                        rotated(t - 1)
                    if M["layer"] == 0 and t > 6:
                        search_steps(3)

            def values_in(M):
                for i, (g, tb) in enumerate(M["v_units"]):
                    if tb == 4 and M["chunk"] + M["ntiles"] // 2 + g + 2 < M["out_chunk"]:
                        split(M["chunk"] + M["ntiles"] // 2 + g + 2)

            def spread(buf, parts, at, step):
                return buf[parts, at:at + (NSAMP - 1) * step + 1:step]

            def place_rows(k):
                kind, layer = ROW_KIND[k], ROW_LAYER[k]
                dve.wait_ge(q_zeroed, Q_ZEROED[k])
                lo, hi = slice(0, 64), slice(64, P)
                if kind == "a":
                    for t, (ha, hb) in enumerate(PAIRS_A):
                        for parts, h in ((lo, ha), (hi, hb)):
                            dve.tensor_copy(spread(qblk, parts, (t // 3) * NSAMP * ROWS_A + h, ROWS_A + 12),
                                            a_tiles[6 + t][parts, SEQ:T]).then_inc(q_placed, 1)
                else:
                    to = qmem if kind == "mem" else qblk
                    for t in range(2 if kind == "mem" else 6):
                        src = (a_tiles[mixers[layer]["mem_q"] + t]) if kind == "mem" else b_tiles[t]
                        for half, parts in enumerate((lo, hi)):
                            dve.tensor_copy(spread(to, parts, t * NSAMP * ROWS_4 + 2 * (t % 2) + half, ROWS_4 + 4),
                                            src[parts, SEQ:T]).then_inc(q_placed, 1)

            def attend(us, extra=None):
                def masked(q):
                    u, col = q["u"], q["u"] % 4
                    dve.wait_ge(s_ready, u + 1)
                    if q["before"]:
                        dve.wait_ge(pt_ready, q["before"]["groups"][-1][0] + 1)
                    if u >= 4:
                        dve.wait_ge(p_ready, u - 3)
                    w, s0 = q["cols"], q["s0"]
                    out, src = pbuf[:, s0:s0 + w], psf[:, s0:s0 + w]
                    if q["kind"] == "mem":
                        dve.tensor_scalar(out, src, 1.0, TAKEN, ALU.mult, ALU.max, accum_out=stats[:, 0, col:col + 1])\
                           .then_inc(s_masked, 1)
                    elif q["kind"] == "a" and q["blk"] == 0:
                        dve.tensor_tensor_reduce(out, src, causal[:, :], 1.0, NEG, ALU.add, ALU.max,
                                                 stats[:, 0, col:col + 1]).then_inc(s_masked, 1)
                    else:
                        if q["kind"] == "a":
                            search_steps((TOPK_PROMPT // 8 + 1) * q["blk"] - searched[0])
                            dve.wait_ge(mask_ready, q["blk"])
                            mask = a_maskb[:, SC0[q["blk"]]:SC0[q["blk"]] + w]
                        else:
                            dve.wait_ge(bmask_loaded[q["blk"] % 2], 16 * (q["blk"] // 2 + 1))
                            mask = b_mask[q["blk"] % 2]
                        dve.tensor_tensor_reduce(out, src, mask, 1.0, NEG, ALU.add, ALU.max,
                                                 stats[:, 0, col:col + 1]).then_inc(s_masked, 1)
                    dve.wait_ge(s_masked, u + 1)
                    dve.tensor_scalar(stats[:, 1, col:col + 1], stats[:, 0, col:col + 1], -SCALE, None, ALU.mult)\
                       .then_inc(nmax_ready, 1)

                def inverse(q):
                    col = q["u"] % 4
                    dve.wait_ge(exp_ready, q["u"] + 1)
                    dve.reciprocal(stats[:, 3, col:col + 1], stats[:, 2, col:col + 1]).then_inc(den_ready, 1)

                def store(q):
                    dve.wait_ge(pv_done, q["groups"][-1][0] + 1)
                    b = q["blk"]
                    cols = slice(b, SEQ, 4) if q["kind"] == "b" else slice(b * P, (b + 1) * P)
                    dve.tensor_copy(ot[:, q["out"], cols], ps[:, 6 + q["pair"] % 2, 0:P]).then_inc(o_stored, 1)

                masked(us[0])
                masked(us[1])
                inverse(us[0])
                for k, q in enumerate(us):
                    if k + 1 < len(us):
                        inverse(us[k + 1])
                    if k + 2 < len(us):
                        masked(us[k + 2])
                    if k >= 2 and us[k - 2]["half"] == 1:
                        store(us[k - 2])
                    if extra:
                        extra(k)
                for q in us[-2:]:
                    if q["half"] == 1:
                        store(q)

            chained = [0]

            def chain(ins):
                ins.then_inc(chain_done, 1)
                chained[0] += 1

            def settle():
                dve.wait_ge(chain_done, chained[0])

            def search_operands(which):
                if which < 4:
                    cols = slice(SC0[which], SC0[which] + (which + 1) * P)
                    return (a_sc[:, cols], tkw[:, 0:(which + 1) * P], a_maskb[:, cols], TOPK_PROMPT,
                            tk[:, which, :])
                return (scs[0:8, 0:PAST + 1], work[0:8, 0:PAST + 1], a_sc[0:8, 0:PAST + 1], TOPK_SAMPLE, tk[0:8, 0, :])

            def find(which, r):
                sc, wk, _, k, found = search_operands(which)
                settle()
                chain(dve.max(found[:, 0:8], sc if r == 0 else wk))
                if r < k // 8 - 1:
                    settle()
                    chain(dve.match_replace(wk, found[:, 0:8], sc if r == 0 else wk, TAKEN))

            def select(which):
                sc, wk, out, k, found = search_operands(which)
                least, count, need = found[:, 7:8], found[:, 8:9], found[:, 9:10]
                settle()
                chain(dve.tensor_scalar(out, sc, least, 0.0, ALU.is_gt, ALU.add, accum_out=count))
                settle()
                chain(dve.tensor_scalar(need, count, -1.0, float(k), ALU.mult, ALU.add))
                chain(dve.tensor_scalar(sc, sc, least, None, ALU.is_equal))
                settle()
                chain(dve.tensor_tensor_scan(wk, sc, sc, 0.0, ALU.add, ALU.max))
                settle()
                chain(dve.scalar_tensor_tensor(wk, wk, need, sc, ALU.is_le, ALU.mult))
                settle()
                chain(dve.tensor_tensor(out, out, wk, ALU.add))
                settle()
                if which < 4:
                    dve.tensor_scalar(out, out, -1.0, -NEG, ALU.add, ALU.mult).then_inc(mask_ready, 1)
                else:
                    chain(dve.tensor_scalar(sc, out, -1.0, -NEG, ALU.add, ALU.mult))
                    settle()
                    chain(dve.tensor_copy(found[:, 0:1], scs[0:8, PAST:PAST + 1]))
                    settle()
                    dve.tensor_scalar(scs[0:8, PAST:COLS_A], offm, found[:, 0:1], None, ALU.add)\
                       .then_inc(mask_ready, 1)

            searched = [0]

            def search_steps(count=SEARCH_STEPS):
                per = TOPK_PROMPT // 8 + 1
                end = min(searched[0] + max(count, 0), SEARCH_STEPS)
                for at in range(searched[0], end):
                    which, r = (1 + at // per, at % per) if at < 3 * per else (4, at - 3 * per)
                    if r < (per - 1 if which < 4 else TOPK_SAMPLE // 8):
                        find(which, r)
                    else:
                        select(which)
                searched[0] = end

            def indexer():
                dve.wait_ge(roped, 5)
                dve.wait_ge(q_zeroed, Q_ZEROED["idx"])
                for h in range(8):
                    for odd in range(2):
                        at = 8 * odd + h
                        dve.tensor_copy(qmem[64 * odd:64 * odd + 64, at:at + 3 * 80 + 1:80],
                                        a_tiles[h // 2][64 * (h % 2):64 * (h % 2) + 64, SEQ + odd:T:2]).then_inc(q_placed, 1)
                dve.wait_ge(iw_ready, 1)
                dve.scalar_tensor_tensor(iws[:, :], ps[0:64, 5, 0:8], IDX_SCALE, selm, ALU.mult, ALU.mult)\
                   .then_inc(iw_done, 1)
                dve.wait_ge(iw_done, 2)
                k = 0
                for blk in range(1, NBLK):
                    sc = a_sc[:, SC0[blk]:SC0[blk] + (blk + 1) * P]
                    for h in range(8):
                        dve.wait_ge(ix_relu, k + 1)
                        r, w = tg[:, k % 2, 0:(blk + 1) * P], iwt[:, blk, h:h + 1]
                        if h == 0:
                            dve.tensor_scalar(sc, r, w, None, ALU.mult).then_inc(ix_added, 1)
                        else:
                            dve.wait_ge(ix_added, k)
                            dve.scalar_tensor_tensor(sc, r, w, sc, ALU.mult, ALU.add).then_inc(ix_added, 1)
                        k += 1
                    dve.wait_ge(ix_added, k)
                    own = a_sc[:, SC0[blk] + blk * P:SC0[blk] + (blk + 1) * P]
                    chain(dve.tensor_tensor(own, own, causal[:, :], ALU.add))
                dve.wait_ge(six_sum, 1)
                dve.tensor_copy(scs[0:8, 0:PAST], psf[0:8, 2048:2048 + PAST]).then_inc(six_done, 1)
                dve.tensor_tensor_reduce(tk[0:8, 1, 0:8], ps[0:8, 6, 0:8], ident[0:8, 0:8], 1.0, 0.0, ALU.mult, ALU.add,
                                         scs[0:8, PAST:PAST + 1]).then_inc(six_done, 1)
                dve.wait_ge(six_done, 2)
                dve.tensor_copy(tk[0:8, 1, 8:9], scs[0:8, PAST:PAST + 1]).then_inc(six_done, 1)
                dve.wait_ge(six_done, 3)

            def rows_of(k):
                kind = ROW_KIND[k]
                rows, cols, nh = nrows(kind), row_cols(kind), nrows(kind) // NSAMP
                if kind == "mem":
                    dve.wait_ge(r_used, max(it["r"] for it in items if it["kind"] == "mem" and it["what"] == "key"
                                            and it["layer"] == ROW_LAYER[k]) + 1)
                else:
                    if kind == "a":
                        search_steps()
                    dve.wait_ge(row_ready, k // 2 + 1)
                chain(dve.reduce_max(rstat[0:rows, 0:1], psf[0:rows, 0:cols], AX_X))
                settle()
                dve.tensor_scalar(rstat[0:rows, 1:2], rstat[0:rows, 0:1], -SCALE, None, ALU.mult).then_inc(row_max, 1)
                dve.wait_ge(row_exp, k + 1)
                chain(dve.reciprocal(rstat[0:rows, 3:4], rstat[0:rows, 2:3]))
                settle()
                dve.tensor_scalar(rowp[0:rows, 0:cols], rowp[0:rows, 0:cols], rstat[0:rows, 3:4], None, ALU.mult)\
                   .then_inc(row_norm, 1)
                last = max(it["r"] for it in items if it["kind"] == kind and it["layer"] == ROW_LAYER[k])
                dve.wait_ge(r_used, last + 1)
                M = mixers[ROW_LAYER[k]]
                tiles_ = PAIRS_A if kind == "a" else [(0, 1), (2, 3)]
                for t, (ha, hb) in enumerate(tiles_):
                    p = t // 3 if kind == "a" else t
                    to = t if kind != "mem" else (6 if M["layer"] == 0 else 2) + t
                    for parts, h in ((slice(0, 64), ha), (slice(64, P), hb)):
                        c = dve.tensor_copy(ot[parts, to, SEQ:T], ps[parts, 6 + p, h:h + (NSAMP - 1) * nh + 1:nh])
                c.then_inc(rowo_stored, 1)

            def tiles_out(M):
                split(M["out_chunk"])
                split(M["out_chunk"] + 1)
                for kt in range(M["out_kt"]):
                    dve.wait_ge(ot_head, M["ot0"] + kt + 1)
                    dve.tensor_tensor(actl[:, kt, :], ot[:, kt, :], acth[:, kt, :].bitcast(F32), ALU.subtract)\
                       .then_inc(ot_rest, 1)
                for m in range(KT):
                    done, count = out_done(M, m)
                    add_out(1.0, m, M["acc"], done, count)
                    if (m + 1) % out_tiles_per_chunk(M) == 0:
                        split(M["out_chunk"] + m // out_tiles_per_chunk(M) + 2)
                    if m == 0:
                        dve.wait_ge(ot_rest, M["ot0"] + M["out_kt"])
                    prepare(M["norm"] + 1, m)

            A, B = mixers
            dve.wait_ge(const_loaded, 16 * 4)
            dve.wait_ge(mem_loaded, 16)
            memory_keys_values()
            ffn(0)
            dve.wait_ge(rope_loaded, 16 * 4)
            tiles_in(A, 0, 6)
            indexer()
            tiles_in(A, 6, 16)
            values_in(A)
            place_rows(0)
            attend(units[0][:16], lambda k: search_steps(1))
            search_steps(5)
            rows_of(0)
            attend(units[0][16:], lambda k: search_steps(1 if k >= 24 else 0))
            place_rows(1)
            rows_of(1)
            tiles_out(A)
            ffn(1)
            ffn(2)
            tiles_in(B, 0, 14)
            values_in(B)
            place_rows(2)
            attend(units[1][:16])
            rows_of(2)
            place_rows(3)
            attend(units[1][16:])
            rows_of(3)
            tiles_out(B)
            ffn(3)
            invert(6)
            dve.wait_ge(rstd_ready, 7)
            for m in range(KT):
                dve.scalar_tensor_tensor(y[:, m, :], y[:, m, :], gains[:, 6, m:m + 1], rstd[:, :], ALU.mult, ALU.mult)\
                   .then_inc(fin_ready, 1)

        @block.gpsimd
        def _(pool):
            def zero(k, buf):
                pool.memset(buf[:, :], 0.0).then_inc(q_zeroed, 1)

            def sum_squares(norm, first, last, i=None):
                for m in range(first, last):
                    more = 0 if i is None else 2 * i
                    pool.wait_ge(sq_ready, more + (KT * norm + m + 1))
                    if m == 0 and i is None:
                        pool.tensor_copy(ssum[:, :], tu[:, 0, :]).then_inc(ssum_done, 1)
                    else:
                        pool.wait_ge(ssum_done, more + (KT * norm + m))
                        pool.tensor_tensor(ssum[:, :], ssum[:, :], tu[:, m % 2, :], ALU.add).then_inc(ssum_done, 1)

            def ffn(f):
                g = FT * f
                for h in range(2):
                    with pool.Fori(0, HALF_TILES[h] // 2) as i:
                        for b in range(2):
                            pool.wait_ge(act_head, 2 * i + (g + b + 1))
                            at = bass.ds(2 * i + b, 1)
                            pool.tensor_tensor(actl[:, at, :].rearrange("p a t -> p (a t)"), tg[:, b, :],
                                               acth[:, at, :].rearrange("p a t -> p (a t)").bitcast(F32), ALU.subtract)\
                                .then_inc(act_rest, 1)
                    g += HALF_TILES[h]
                norm = [1, 3, 4, 6][f]
                sum_squares(norm, 0, 2)
                with pool.Fori(1, KT // 2) as i:
                    sum_squares(norm, 0, 2, i)

            def ropes(M):
                for j, t in enumerate(M["roped"]):
                    k = M["rope0"] + j
                    tile = M["tiles"][t]
                    pool.wait_ge(rot_ready, k + 1)
                    pool.tensor_tensor(tile, tile, cosf[:, :], ALU.mult).then_inc(cos_ready, 1)
                    pool.wait_ge(cos_ready, k + 1)
                    pool.wait_ge(sin_ready, k + 1)
                    pool.tensor_tensor(tile, tile, tg[:, k % 2, :], ALU.add).then_inc(roped, 1)

            def diagonals(us):
                for q in us:
                    pool.wait_ge(den_ready, q["u"] + 1)
                    pool.tensor_scalar(diag[:, q["u"] % 4, :], ident[:, :], stats[:, 3, q["u"] % 4:q["u"] % 4 + 1], None,
                                       ALU.mult).then_inc(p_ready, 1)

            A, B = mixers
            sum_squares(0, 0, KT)
            ffn(0)
            pool.wait_ge(rms_ready, 2)
            zero("idx", qmem)
            pool.wait_ge(rope_loaded, 16 * 4)
            ropes(A)
            pool.wait_ge(r_used, 2)
            zero(0, qmem)
            diagonals(units[0][:16])
            zero(1, qblk)
            diagonals(units[0][16:])
            sum_squares(2, 0, KT)
            ffn(1)
            ffn(2)
            pool.wait_ge(rms_ready, 5)
            zero(2, qmem)
            zero(3, qblk)
            ropes(B)
            diagonals(units[1])
            sum_squares(5, 0, KT)
            ffn(3)


def kernel(x_prompt, x_sample, cache_kv_a, cache_kidx_a, state_kv_b1, state_kv_b2, state_kv_b3, cache_mem_kv,
           page_table, mem_prompt, ffn_norm, w_ffn_in, w_ffn_out, mix_norm, mem_norm, w_mem_kv, w_in_a, w_out_a,
           w_in_b, w_out_b, final_norm):
    import numpy as np
    from concourse import bacc
    from concourse.bass_utils import run_bass_kernel_spmd

    f32 = np.float32
    a = {}

    def feature_major(x):
        return np.ascontiguousarray(np.asarray(x).T.reshape(KT, P, -1).transpose(1, 0, 2))

    def chunks(w, cols, k_tiles, width):
        w = np.concatenate([np.asarray(w), np.zeros((w.shape[0], 1), f32)], axis=1)[:, cols]
        w = w.reshape(k_tiles, P, -1, width * P).transpose(2, 1, 0, 3)
        return np.ascontiguousarray(w.reshape(w.shape[0], P, -1))

    xs = np.concatenate([np.asarray(x_prompt)[0], np.asarray(x_sample)[:, 0]], axis=0)
    a["x"] = feature_major(xs)
    a["mem_x"] = feature_major(np.asarray(mem_prompt)[0])
    norms = [ffn_norm[0, 0], mix_norm[0], ffn_norm[0, 1], ffn_norm[1, 0], mix_norm[1], ffn_norm[1, 1], final_norm,
             mem_norm[0], mem_norm[1]]
    a["gains"] = np.ascontiguousarray(np.stack([np.asarray(g).reshape(KT, P) for g in norms]).transpose(2, 0, 1))
    w = np.asarray(w_ffn_in).reshape(NFFN, KT, P, 2, FT, P)
    a["w_ffn_in"] = np.ascontiguousarray(w.transpose(0, 4, 2, 1, 3, 5).reshape(NFFN * FT, P, CH))
    w = np.asarray(w_ffn_out).reshape(NFFN, FT, P, KT, P).transpose(0, 3, 2, 1, 4)
    w = w.reshape(NFFN * KT, P, FT, P)
    a["w_ffn_out0"] = np.ascontiguousarray(w[:, :, :HALF_TILES[0]]).reshape(NFFN * KT, P, -1)
    a["w_ffn_out1"] = np.ascontiguousarray(w[:, :, HALF_TILES[0]:]).reshape(NFFN * KT, P, -1)
    half = 4 * HD
    a["w_mem"] = np.concatenate([chunks(np.asarray(w_mem_kv)[i], np.arange(2 * half), KT, 2) for i in range(2)])

    def head(base, h):
        return base + h * HD + np.arange(HD)
    q0, k0, v0, iq0, ik0, iw0, mq0 = 0, 768, 1024, 1280, 1792, 1856, 1864
    cols = [iq0 + np.arange(512), ik0 + np.arange(HD), ik0 + np.arange(HD), iw0 + np.arange(8), np.full(P - 8, -1)]
    cols += [np.concatenate([head(q0, x), head(q0, z)]) for x, z in PAIRS_A]
    cols += [k0 + np.arange(half), mq0 + np.arange(half), v0 + np.arange(half)]
    a["w_in_a"] = chunks(np.asarray(w_in_a)[0], np.concatenate(cols), KT, 2)
    group = lambda g, part: (3 * g + part) * half + np.arange(half)
    cols = [group(g, part) for part in (0, 1) for g in range(3)] + [9 * half + np.arange(half)]
    cols += [group(g, 2) for g in range(3)]
    a["w_in_b"] = chunks(np.asarray(w_in_b)[0], np.concatenate(cols), KT, 2)
    order = np.concatenate([np.concatenate([head(0, x), head(0, z)]) for x, z in PAIRS_A] + [768 + np.arange(half)])
    a["w_out_a"] = chunks(np.asarray(w_out_a)[0][order], np.arange(D), 8, 2)
    a["w_out_b"] = chunks(np.asarray(w_out_b)[0], np.arange(D), 4, 4)

    pool = np.asarray(cache_kv_a)[0]
    n_pool = pool.shape[0]
    a["kpool"] = np.ascontiguousarray(pool[:, :, 0].reshape(n_pool, PAGE, 2, P).transpose(0, 3, 2, 1)).reshape(n_pool, P, 256)
    a["vpool"] = np.ascontiguousarray(pool[:, :, 1].reshape(n_pool, PAGE, 256))
    a["kidx"] = np.ascontiguousarray(np.asarray(cache_kidx_a)[0].transpose(0, 2, 1))
    a["pages"] = np.asarray(page_table).reshape(1, -1).astype(np.int32)

    def keys(c):
        b, n = c.shape[:2]
        return c.reshape(b, n, 2, P).transpose(0, 3, 2, 1)

    def by_items(c, per):
        return np.ascontiguousarray(c.reshape(NSAMP // per, per, P, -1).transpose(0, 2, 1, 3)).reshape(NSAMP // per, P, -1)

    mem = np.asarray(cache_mem_kv)
    per = ITEMS["mem"][0]
    a["mem_key"] = np.stack([by_items(keys(mem[i, :, :, 0]), per) for i in range(2)])
    a["mem_value"] = np.stack([by_items(mem[i, :, :, 1].reshape(NSAMP, 2, P, 256).transpose(0, 2, 1, 3), per)
                               for i in range(2)])
    states = [np.asarray(s)[0] for s in (state_kv_b1, state_kv_b2, state_kv_b3)]
    seen = [states[0], states[1][:, ::4], states[2][:, ::16]]
    per = ITEMS["b"][0]
    a["b_key"] = by_items(np.concatenate([keys(s[:, :, 0]).reshape(NSAMP, P, -1) for s in seen], axis=2), per)
    vals = [np.pad(s[:, :, 1].reshape(NSAMP, s.shape[1], 256), ((0, 0), (0, P - s.shape[1]), (0, 0))) for s in seen]
    a["b_value"] = by_items(np.stack(vals, axis=2), per)
    a["state0"] = np.ascontiguousarray(states[0][:, 1:]).reshape(NSAMP, 127, 512)
    a["state1"] = np.ascontiguousarray(states[1][:, 1:]).reshape(NSAMP, 511, 512)
    a["state2"] = np.ascontiguousarray(states[2]).reshape(NSAMP, 1024, 512)

    rot_half = HD // 8
    inv = (500000.0 ** (-np.arange(rot_half, dtype=np.float64) / rot_half)).astype(f32)
    pos = np.concatenate([np.arange(SEQ), np.full(NSAMP, PAST)]).astype(f32)
    ang = (pos[:, None] * inv[None, :]).astype(np.float64)
    cos, sin = np.ones((P, T), f32), np.zeros((P, T), f32)
    rot = np.zeros((P, P), f32)
    for h in (0, HD):
        for i in range(rot_half):
            cos[h + i] = cos[h + rot_half + i] = np.cos(ang[:, i])
            sin[h + i], sin[h + rot_half + i] = -np.sin(ang[:, i]), np.sin(ang[:, i])
            rot[h + rot_half + i, h + i] = rot[h + i, h + rot_half + i] = 1.0
    a["cos"], a["sin"], a["rot"], a["ident"] = cos, sin, rot, np.eye(P, dtype=f32)
    a["eps"] = np.full((P, 1), EPS, f32)
    a["causal"] = np.where(np.arange(P)[None, :] <= np.arange(P)[:, None], 0.0, NEG).astype(f32)
    small = np.zeros((P, 264), f32)
    for b in range(NSAMP):
        small[0:8, b * 8:b * 8 + 8] = np.eye(8)
        small[b * 8:b * 8 + 8, 64 + b] = 1.0
        small[b, 128 + b * 12:128 + (b + 1) * 12] = 1.0
    small[0:8, 224:232] = np.where(np.eye(8) > 0, 0.0, NEG)
    for r in range(32):
        for g in range(3):
            small[r, 232 + 8 * g:240 + 8 * g] = np.where(np.arange(8) == r // 4, 0.0, NEG)
    a["small"] = small
    masks = np.full((4, P, 768), NEG, f32)
    q, s = np.arange(P)[:, None], np.arange(SEQ)[None, :]
    for r in range(4):
        back = r + 4 * q - s
        masks[r, :, 0:SEQ][(back >= 0) & (back <= WINDOWS[0][0])] = 0.0
        back = q - np.arange(P)[None, :]
        masks[r, :, SEQ:SEQ + P][back >= 0] = 0.0
        masks[r, :, SEQ + P:][(back >= 0) & (back % 4 == 0)] = 0.0
    a["mask_b"] = masks

    out_shapes = {"y": (P, KT, T), "memk": (P, 2, 2, MEM), "memv": (P, 2, 2, MEM), "k_a": (P, 2, T),
                  "v_a": (P, NBLK, 256), "vs_a": (8, 256), "kidx": (64, T), "k_b": (P, 6, T),
                  "v_b": (P, 3, NBLK, 256), "vs_b": (8, 3, 256), "state0": (NSAMP, 127, 512),
                  "state1": (NSAMP, 511, 512), "state2": (NSAMP, 1024, 512)}
    nc = bacc.Bacc("TRN2", target_bir_lowering=False, num_devices=1)
    ins = {k: nc.dram_tensor(f"in_{k}", v.shape, mybir.dt.from_np(v.dtype), kind="ExternalInput").ap() for k, v in a.items()}
    outs = {k: nc.dram_tensor(f"out_{k}", s, F32, kind="ExternalOutput").ap() for k, s in out_shapes.items()}
    build(nc, ins, outs)
    r = run_bass_kernel_spmd(nc, [{f"in_{k}": v for k, v in a.items()}], core_ids=[0]).results[0]
    r = {k: np.asarray(r[f"out_{k}"]) for k in out_shapes}

    yt = r["y"].transpose(2, 1, 0).reshape(T, D)
    y_prompt, y_sample = yt[None, :SEQ], yt[SEQ:, None]
    mk = r["memk"].transpose(1, 3, 2, 0).reshape(2, MEM, 4, HD)
    mv = r["memv"].transpose(1, 2, 0, 3).reshape(2, MEM, 4, HD)
    new_mem = np.stack([mk, mv], axis=2)[:, None]
    ka = r["k_a"].transpose(2, 1, 0).reshape(T, 4, HD)
    va = np.concatenate([r["v_a"].transpose(1, 0, 2).reshape(SEQ, 4, HD), r["vs_a"].reshape(8, 4, HD)])
    kv_a = np.stack([ka, va], axis=1)
    kidx = r["kidx"].T
    kb = r["k_b"].reshape(P, 3, 2, T).transpose(1, 3, 2, 0).reshape(3, T, 4, HD)
    vb = r["v_b"].transpose(1, 2, 0, 3)
    vb = np.stack([vb[0].reshape(SEQ, 256)] + [vb[g].transpose(1, 0, 2).reshape(SEQ, 256) for g in (1, 2)])
    vb = np.concatenate([vb, r["vs_b"].transpose(1, 0, 2)], axis=1).reshape(3, T, 4, HD)
    kv_b = np.stack([kb, vb], axis=2)
    new_b_prompt = [kv_b[g, SEQ - min(w, SEQ):SEQ][None, None] for g, (w, _) in enumerate(WINDOWS)]
    new_b_sample = [np.concatenate([r[f"state{g}"].reshape(NSAMP, -1, 2, 4, HD), kv_b[g, SEQ:, None]], axis=1)[None]
                    for g in range(3)]
    return (y_prompt, y_sample, kv_a[None, None, :SEQ], kidx[None, None, :SEQ], *new_b_prompt, new_mem,
            kv_a[None, SEQ:, None], kidx[None, SEQ:, None], *new_b_sample)
```

```python
from contextlib import ExitStack

import concourse.bass as bass
from concourse import mybir

F32 = mybir.dt.float32
F32R = mybir.dt.float32r
I32 = mybir.dt.int32
ALU = mybir.AluOpType
ACT = mybir.ActivationFunctionType
AX_X = mybir.AxisListType.X

P = 128
D = 1024
KT = D // P
SEQ, NSAMP = 512, 8
T = SEQ + NSAMP
TH = T // 2
NBLK = SEQ // P
FF = 2816
FT = FF // P
HALF_TILES = (12, FT - 12)
HD = 64
MEM = 256
PAST, PAGE = 1024, 128
NPAGE = PAST // PAGE
TOPK_PROMPT, TOPK_SAMPLE = 128, 256
SCALE = HD ** -0.5
IDX_SCALE = float((8 * 64) ** -0.5)
EPS = 1e-6
NEG = -1e30
TAKEN = -3e38
CH = 2048
NFFN = 4
FFN_CHUNKS = FT + 2 * KT

ROWS_A, ROWS_4 = NSAMP * 12, NSAMP * 4
PAIRS_A = [(0, 3), (1, 4), (2, 5), (6, 9), (7, 10), (8, 11)]
WINDOWS = [(128, 1), (512, 4), (2048, 16)]
KEYS_B = [128, 128, 64]
COLS_A = PAST + NSAMP
COLS_B = sum(KEYS_B) + 3 * NSAMP
SLOTS = 6
ITEMS = {"idx": (4, 2 * PAST, 0), "a": (1, 2 * PAST, 2 * PAST), "mem": (4, 2 * MEM, 2 * MEM), "b": (2, 640, 768)}


def chunk_plan():
    plan, n = {}, 0
    for name, count in (("mem", 4), ("ffn0", FFN_CHUNKS), ("in_a", 9), ("out_a", 4), ("ffn1", FFN_CHUNKS),
                        ("ffn2", FFN_CHUNKS), ("in_b", 10), ("out_b", 2), ("ffn3", FFN_CHUNKS)):
        plan[name] = n
        n += count
    return plan, n


def ring_plan():
    items, loads, last = [], [0] * SLOTS, [None] * SLOTS
    for what, kind, layer in (("key", "idx", 0), ("key", "mem", 0), ("key", "a", 0), ("value", "mem", 0),
                              ("value", "a", 0), ("key", "mem", 1), ("key", "b", 1), ("value", "mem", 1),
                              ("value", "b", 1)):
        per = ITEMS[kind][0]
        for first in range(0, NSAMP, per):
            r = len(items)
            slot = r if kind == "idx" else (r - 2) % SLOTS
            dmas = per * NPAGE if kind in ("idx", "a") else 1
            loads[slot] += 16 * dmas
            items.append(dict(what=what, kind=kind, layer=layer, first=first, r=r, slot=slot, loaded=loads[slot],
                              after=last[slot]))
            last[slot] = r
    return items


def units_a():
    units = units_mem(6)
    for blk in range(NBLK):
        for tile, pair in enumerate(PAIRS_A):
            for half in range(2):
                units.append(dict(kind="a", blk=blk, tile=tile, half=half, cols=(blk + 1) * P,
                                  kv=2 * (tile // 3) + half, out=tile))
    return units


def units_mem(first_out):
    return [dict(kind="mem", blk=blk, tile=tile, half=half, cols=MEM, kv=2 * tile + half, out=first_out + tile)
            for blk in range(NBLK) for tile in range(2) for half in range(2)]


def units_b():
    return [dict(kind="b", blk=r, tile=tile, half=half, cols=768, kv=2 * tile + half, out=tile)
            for r in range(4) for tile in range(2) for half in range(2)]


def build(nc, ins, outs):
    plan, n_chunks = chunk_plan()
    with ExitStack() as ctx:
        def sb(name, shape, dt=F32):
            return ctx.enter_context(nc.sbuf_tensor(name, shape, dt))

        def sem(name):
            return ctx.enter_context(nc.semaphore(name))

        arena_at = (nc.sbuf_base + 31) // 32 * 32
        arena = sb("arena", [P, (2 * KT + 24) * T + 4 * CH])

        def placed(name, shape, dt, at):
            return nc.alloc_sbuf_tensor_at(name, shape, dt, offset=arena_at + 4 * at)

        y = sb("y", [P, KT, T])
        X_AT, ACT_AT, W_AT = 0, 2 * KT * T, (2 * KT + 24) * T
        xh = placed("xh", [P, KT, T], F32R, X_AT)
        xl = placed("xl", [P, KT, T], F32R, X_AT + KT * T)
        acth = placed("acth", [P, 12, T], F32R, ACT_AT)
        actl = placed("actl", [P, 12, T], F32R, ACT_AT + 12 * T)
        raw = sb("raw", [P, 2, CH])
        wh = placed("wh", [P, 2, CH], F32R, W_AT)
        wl = placed("wl", [P, 2, CH], F32R, W_AT + 2 * CH)
        tg = sb("tg", [P, 2, T])
        tu = sb("tu", [P, 2, T])
        rstd = sb("rstd", [P, T])
        ssum = sb("ssum", [P, T])
        qmem = ssum[:, 0:2 * ROWS_4 * NSAMP]
        rtok = sb("rtok", [P, 9])
        memk = sb("memk", [P, 2, 2, MEM])
        memv = sb("memv", [P, 2, 2, MEM])
        gains = sb("gains", [P, 9, KT])
        cosf = sb("cosf", [P, T])
        sinf = sb("sinf", [P, T])
        rot = sb("rot", [P, P])
        ident = sb("ident", [P, P])
        ones = sb("ones", [P, P])
        causal = sb("causal", [P, P])
        small = sb("small", [P, 64 + 64 + 96 + 8 + 32])
        stats = sb("stats", [P, 4, 4])
        rstat = sb("rstat", [P, 2, 4])
        tk = sb("tk", [P, 4, 10])
        iwt = sb("iwt", [P, NBLK, 8])
        iws = sb("iws", [64, 8])
        scs = sb("scs", [P, COLS_A])
        work = sb("work", [P, COLS_A])
        tkw = sb("tkw", [P, 768])
        qblk = sb("qblk", [P, 2 * ROWS_A * NSAMP])
        ring = sb("ring", [P, 2, CH])
        ring_w = placed("ring_w", [P, 4, CH], F32, W_AT)
        pages = sb("pages", [1, NSAMP * NPAGE], I32)
        epsb = sb("epsb", [P, 1])

        e8, selm, e96, offm, offb = (small[0:8, 0:64], small[0:64, 64:72], small[0:8, 128:224],
                                     small[0:8, 224:232], small[0:32, 232:256])
        tiles = placed("tiles", [P, 16, T], F32, ACT_AT)
        VALUES_AT = ACT_AT + 16 * T
        a_tiles = [tiles[:, i, :] for i in range(16)]
        a_v = placed("a_v", [P, NBLK, 256], F32, VALUES_AT)
        a_vs = placed("a_vs", [8, 256], F32, VALUES_AT + 3584)
        a_maskb = placed("a_maskb", [P, 1152], F32, VALUES_AT + 1280)
        a_sc = placed("a_sc", [P, 1152], F32, VALUES_AT + 2432)
        b_tiles = a_tiles[:14]
        b_v = placed("b_v", [P, 3, NBLK, 256], F32, VALUES_AT)
        b_vs = placed("b_vs", [8, 3, 256], F32, VALUES_AT + 3072)
        b_mask = [scs[:, 0:768], tkw[:, 0:768]]
        pbuf = placed("pbuf", [P, 2048], F32, X_AT)
        ptb = placed("ptb", [P, 2, 512], F32, X_AT + 2048)
        diag = placed("diag", [P, 4, P], F32, X_AT + 3072)
        rowp = [tu[:, 0, 0:MEM], placed("rowp", [P, COLS_A], F32, X_AT)]
        rowt = [placed("rowt_mem", [P, 2, ROWS_4], F32, X_AT + 3968),
                placed("rowt", [P, 9, ROWS_A], F32, X_AT + 1040)]
        rowo = placed("rowo", [P, NSAMP * 256], F32, X_AT + 1904)
        rown = tu[:, 1, 0:2 * ROWS_A].rearrange("p (t r) -> p t r", t=2)
        OUT_AT = [96, 0]
        ot = placed("ot", [P, KT, T], F32, X_AT + KT * T)
        mraw = placed("mraw", [P, KT, MEM], F32, ACT_AT)
        mh = [placed("mh0", [P, KT, MEM], F32R, ACT_AT + 2048),
              placed("mh1", [P, KT, MEM], F32R, ACT_AT + 8720)]
        ml = [placed("ml0", [P, KT, MEM], F32R, ACT_AT + 4096),
              placed("ml1", [P, KT, MEM], F32R, ACT_AT + 6144)]
        msq = placed("msq", [P, KT, MEM], F32, ACT_AT + 6144)
        msum = placed("msum", [P, MEM], F32, ACT_AT + 8192)
        mrstd = placed("mrstd", [P, MEM], F32, ACT_AT + 8448)
        mrtok = placed("mrtok", [P, 2], F32, ACT_AT + 8704)

        ps = ctx.enter_context(nc.psum_tensor("ps", [P, 8, 512], F32))
        psf = ps[:, :, :].rearrange("p b c -> p (b c)")

        def halves(x):
            return x.rearrange("p (h t) -> p h t", h=2)

        def bank2(b):
            return ps[:, b:b + 2, 0:TH]

        const_loaded = sem("const_loaded"); rope_loaded = sem("rope_loaded")
        y_loaded = sem("y_loaded"); mem_loaded = sem("mem_loaded")
        pages_loaded = sem("pages_loaded"); ones_set = sem("ones_set")
        w_loaded = [sem("w_loaded0"), sem("w_loaded1")]
        w_head = sem("w_head"); w_rest = sem("w_rest"); w_used = sem("w_used")
        x_head = sem("x_head"); x_rest = sem("x_rest"); sq_ready = sem("sq_ready"); ssum_done = sem("ssum_done")
        rms_ready = sem("rms_ready"); rms_read = sem("rms_read"); tok_read = sem("tok_read")
        rstd_ready = sem("rstd_ready"); rtok_ready = sem("rtok_ready")
        gate_ready = sem("gate_ready"); up_ready = sem("up_ready")
        silu_ready = sem("silu_ready"); hid_ready = sem("hid_ready")
        act_head = sem("act_head"); act_rest = sem("act_rest"); y_added = sem("y_added")
        m_head = sem("m_head"); m_rest = sem("m_rest"); m_sq = sem("m_sq"); m_sum = sem("m_sum")
        m_rms = sem("m_rms"); m_sqrt = sem("m_sqrt"); m_rstd = sem("m_rstd"); m_first = sem("m_first")
        mkv_done = sem("mkv_done")
        t_ready = sem("t_ready"); raw_ready = sem("raw_ready"); rot_ready = sem("rot_ready")
        sin_ready = sem("sin_ready"); cos_ready = sem("cos_ready"); roped = sem("roped")
        v_ready = sem("v_ready"); v_done = sem("v_done"); out_first = sem("out_first")
        iw_ready = sem("iw_ready"); iw_done = sem("iw_done")
        ix_ready = sem("ix_ready"); ix_relu = sem("ix_relu"); ix_added = sem("ix_added")
        chain_done = sem("chain_done"); mask_ready = sem("mask_ready")
        six_relu = sem("six_relu"); six_sum = sem("six_sum"); six_done = sem("six_done")
        q_zeroed = sem("q_zeroed"); q_placed = sem("q_placed")
        r_loaded = [sem(f"r_loaded{i}") for i in range(SLOTS)]
        r_used = sem("r_used")
        s_ready = sem("s_ready"); s_masked = sem("s_masked"); nmax_ready = sem("nmax_ready")
        exp_ready = sem("exp_ready"); den_ready = sem("den_ready"); p_ready = sem("p_ready")
        pt_ready = sem("pt_ready"); pt_copied = sem("pt_copied"); pv_done = sem("pv_done"); o_stored = sem("o_stored")
        row_ready = sem("row_ready"); row_max = sem("row_max"); row_exp = sem("row_exp"); row_norm = sem("row_norm")
        rowt_ready = sem("rowt_ready"); rowt_copied = sem("rowt_copied")
        rowv_copied = [sem("rowv_copied0"), sem("rowv_copied1")]
        new_ready = sem("new_ready"); new_copied = sem("new_copied"); rowo_ready = sem("rowo_ready"); rowo_stored = sem("rowo_stored")
        ot_head = sem("ot_head"); ot_rest = sem("ot_rest")
        bmask_loaded = [sem("bmask_loaded0"), sem("bmask_loaded1")]
        out_written = sem("out_written"); fin_ready = sem("fin_ready"); copied = sem("copied")

        units = [units_a(), units_mem(2) + units_b()]
        items = ring_plan()

        ATTEND_AHEAD = {"mem": 3, "a": 3, "b": 2}

        def place(all_units):
            group = 0
            for u, q in enumerate(all_units):
                wide = q["kind"] == "b"
                q.update(u=u, pair=u // 2, s0=(u % 2) * 1024 if wide else (u % 4) * 512, groups=[],
                         size=1024 if wide else 512)
                for at in range(0, q["cols"] // P, 3 if wide else 4):
                    q["groups"].append((group, at, min(3 if wide else 4, q["cols"] // P - at)))
                    group += 1
                q["before"] = next((v for v in reversed(all_units[:u])
                                    if v["s0"] < q["s0"] + q["size"] and q["s0"] < v["s0"] + v["size"]), None)

        place(units[0] + units[1])
        SC0 = {1: 0, 2: 256, 3: 640}
        V_AT = {0: 0, 1: 5}
        A_ROPED = [i for i in range(16) if i not in (5, 14, 15)]
        mixers = [
            dict(layer=0, norm=1, chunk=plan["in_a"], out_chunk=plan["out_a"], ntiles=16, tile0=0, rope0=0,
                 roped=A_ROPED, tiles=a_tiles, v0=0, v_units=[(0, tb) for tb in range(5)], acc=16, out_kt=8, ot0=0,
                 out0=0, mem_q=14),
            dict(layer=1, norm=4, chunk=plan["in_b"], out_chunk=plan["out_b"], ntiles=14, tile0=16, rope0=13,
                 roped=list(range(12)), tiles=b_tiles, v0=5, v_units=[(g, tb) for g in range(3) for tb in range(5)],
                 acc=56, out_kt=4, ot0=9, out0=4, mem_q=12)]
        FFN_ACC = [0, 24, 40, 64]
        FFN_NORM = [0, 2, 3, 5]
        ROW_KIND = ["mem", "a", "mem", "b"]
        ROW_LAYER = [0, 0, 1, 1]
        SEARCH_STEPS = 2 * (3 * (TOPK_PROMPT // 8 + 1) + TOPK_SAMPLE // 8 + 1)
        Q_PLACED = {"idx": 16, 0: 20, 1: 32, 2: 36, 3: 48}
        Q_ZEROED = {1: 1, "idx": 2, 0: 3, 3: 4, 2: 5}

        def slot(i):
            return ring[:, i, :] if i < 2 else ring_w[:, i - 2, :]

        def nrows(kind):
            return ROWS_A if kind == "a" else ROWS_4

        def row_tiles(kind):
            if kind == "a":
                return [(i * P, P) for i in range(NPAGE)] + [(PAST, NSAMP)]
            if kind == "b":
                return [(0, 128), (128, 128), (256, 64)] + [(320 + NSAMP * g, NSAMP) for g in range(3)]
            return [(0, 128), (128, 128)]

        def row_cols(kind):
            return {"a": COLS_A, "b": COLS_B, "mem": MEM}[kind]

        def tokens(tb, g):
            if tb == 4:
                return slice(SEQ, T)
            return slice(tb * P, (tb + 1) * P) if g == 0 else slice(tb, SEQ, 4)

        def rtok_col(tb, g):
            return tb if g == 0 or tb == 4 else 5 + tb

        def tile_done(M, t):
            if t % 2:
                return w_used, M["chunk"] + t // 2 + 1
            return t_ready, (M["tile0"] + t) // 2 + 1

        def v_block_done(M, i):
            if M["v_units"][i][1] == 4:
                return w_used, M["chunk"] + M["ntiles"] // 2 + i // 5 + 1
            return v_ready, 4 * ((M["v0"] + i) // 5) + i % 5 + 1

        def out_tiles_per_chunk(M):
            return CH // (M["out_kt"] * P)

        def out_done(M, m):
            per = out_tiles_per_chunk(M)
            if m % per == per - 1:
                return w_used, M["out_chunk"] + m // per + 1
            return out_first, (0 if M["layer"] == 0 else 4) + m - m // per + 1

        a_items = [it["r"] for it in items if it["kind"] == "a"]
        BY_SCALAR = [a_items[i] for i in (5, 7, 11, 13, 15)]

        def last_in_place(k, n):
            return max(it["r"] for it in items if it["layer"] == ROW_LAYER[k] and it["slot"] in (2 + n % 2, 4 + n % 2))

        LAST_VALUES = [max(it["r"] for it in items if (it["kind"], it["layer"]) == kl) for kl in zip(ROW_KIND, ROW_LAYER)]

        def page_number(eng, at, src):
            return eng.value_load(pages[0:1, at:at + 1], min_val=0, max_val=ins[src].shape[0] - 1)

        def load_pages(eng, it):
            src = "kpool" if it["what"] == "key" else "vpool"
            numbers = [page_number(eng, it["first"] * NPAGE + k, src) for k in range(NPAGE)]
            for k, page in enumerate(numbers):
                eng.dma_start(slot(it["slot"])[:, k * 256:(k + 1) * 256],
                              ins[src][bass.ds(page, 1)].rearrange("a p c -> (a p) c")).then_inc(r_loaded[it["slot"]], 16)

        block = ctx.enter_context(nc.Block())

        @block.sync
        def _(sp):
            sp.dma_start(raw[:, 0, :], ins["w_mem"][0]).then_inc(w_loaded[0], 16)
            sp.dma_start(mraw[:, :, :], ins["mem_x"]).then_inc(mem_loaded, 16)
            for t, src in ((gains[:, :, :], "gains"), (ident[:, :], "ident"), (small[:, :], "small"),
                           (epsb[:, :], "eps")):
                sp.dma_start(t, ins[src]).then_inc(const_loaded, 16)
            sp.dma_start(raw[:, 1, :], ins["w_mem"][1]).then_inc(w_loaded[1], 16)
            sp.dma_start(y[:, :, :], ins["x"]).then_inc(y_loaded, 16)
            for t, src in ((cosf, "cos"), (sinf, "sin"), (rot, "rot"), (causal, "causal")):
                sp.dma_start(t[:, :], ins[src]).then_inc(rope_loaded, 16)
            sp.dma_start(pages[:, :], ins["pages"]).then_inc(pages_loaded, 16)

            def load(n, src):
                sp.wait_ge(w_head, n - 1)
                sp.wait_ge(w_rest, n - 1)
                sp.dma_start(raw[:, n % 2, 0:src.shape[1]], src).then_inc(w_loaded[n % 2], 16)

            def load_loop(n0, src, first, count, cols):
                with sp.Fori(0, count // 2) as i:
                    for b in range(2):
                        sp.wait_ge(w_head, 2 * i + (n0 + b - 1))
                        sp.wait_ge(w_rest, 2 * i + (n0 + b - 1))
                        sp.dma_start(raw[:, (n0 + b) % 2, 0:cols],
                                     src[bass.ds(2 * i + (first + b), 1)].rearrange("a p c -> (a p) c"))\
                            .then_inc(w_loaded[(n0 + b) % 2], 16)

            def ffn_loads(f):
                n = plan[f"ffn{f}"]
                for h in range(2):
                    count = HALF_TILES[h]
                    load_loop(n, ins["w_ffn_in"], f * FT + h * HALF_TILES[0], count, CH)
                    if f == 0:
                        for m in range(KT):
                            load(n + count + m, ins[f"w_ffn_out{h}"][m])
                            index_pages(h * KT + m)
                    else:
                        load_loop(n + count, ins[f"w_ffn_out{h}"], f * KT, KT, count * P)
                    n += count + KT

            def ring_loads(kind, what, layer):
                for it in items:
                    if (it["kind"], it["what"], it["layer"]) != (kind, what, layer) or it["r"] in BY_SCALAR:
                        continue
                    if it["after"] is not None:
                        sp.wait_ge(r_used, it["after"] + 1)
                    if it["slot"] >= 2:
                        sp.wait_ge(w_used, mixers[layer]["out_chunk"])
                    if kind == "a":
                        load_pages(sp, it)
                    else:
                        src = ins[f"{kind}_{what}"] if kind == "b" else ins[f"mem_{what}"][layer]
                        sp.dma_start(slot(it["slot"])[:, 0:src.shape[2]], src[it["first"] // ITEMS[kind][0]])\
                            .then_inc(r_loaded[it["slot"]], 16)

            def index_pages(part):
                b, k0 = part // 2, part % 2 * (NPAGE // 2)
                numbers = [page_number(sp, b * NPAGE + k0 + k, "kidx") for k in range(NPAGE // 2)]
                for k, page in enumerate(numbers):
                    at = (b % 4 // 2 * NPAGE + k0 + k) * P
                    sp.dma_start(ring[64 * (b % 2):64 * (b % 2) + 64, b // 4, at:at + P],
                                 ins["kidx"][bass.ds(page, 1)].rearrange("a p c -> (a p) c")).then_inc(r_loaded[b // 4], 16)

            load(2, ins["w_mem"][2])
            load(3, ins["w_mem"][3])
            sp.wait_ge(pages_loaded, 16)
            ffn_loads(0)
            for i in range(9):
                load(plan["in_a"] + i, ins["w_in_a"][i])
            for i in range(2):
                load(plan["out_a"] + i, ins["w_out_a"][i])
            for what in ("key", "value"):
                for kind in ("mem", "a"):
                    ring_loads(kind, what, 0)
            load(plan["out_a"] + 2, ins["w_out_a"][2])
            load(plan["out_a"] + 3, ins["w_out_a"][3])
            ffn_loads(1)
            ffn_loads(2)
            for i in range(10):
                load(plan["in_b"] + i, ins["w_in_b"][i])
            for i in range(2):
                load(plan["out_b"] + i, ins["w_out_b"][i])
            for r in range(2):
                sp.dma_start(b_mask[r], ins["mask_b"][r]).then_inc(bmask_loaded[r], 16)
            ring_loads("mem", "key", 1)
            ring_loads("b", "key", 1)
            first_b = units[1][16]["u"]
            for r in range(2, 4):
                sp.wait_ge(s_masked, first_b + 4 * (r - 1))
                sp.dma_start(b_mask[r % 2], ins["mask_b"][r]).then_inc(bmask_loaded[r % 2], 16)
            ring_loads("mem", "value", 1)
            ring_loads("b", "value", 1)
            ffn_loads(3)
            for m in range(KT):
                sp.wait_ge(fin_ready, m + 1)
                sp.dma_start(outs["y"][:, m, :], y[:, m, :]).then_inc(out_written, 16)
            sp.wait_ge(out_written, 16 * (2 + 4 + 3 + KT))
            sp.wait_ge(copied, 16 * 3 * NSAMP)

        @block.tensor
        def _(pe):
            def chunk_ready(n):
                pe.wait_ge(w_head, n + 1)
                pe.wait_ge(w_rest, n + 1)

            def product(out, heads, rests, xheads, xrests, nk, before=None):
                for kt in range(nk):
                    if before is not None:
                        before(kt)
                    for i, (w, x) in enumerate(((heads, xheads), (heads, xrests), (rests, xheads))):
                        for o, moving in zip(out, x(kt)):
                            mm = pe.matmul(o, w(kt), moving, start=(kt == 0 and i == 0),
                                           stop=(kt == nk - 1 and i == 2))
                return mm

            def by_halves(buf):
                return lambda kt: [buf[:, kt, h * TH:(h + 1) * TH] for h in range(2)]

            def tile_of(buf, slot, t, width=2):
                return lambda kt: buf[:, slot, (kt * width + t) * P:(kt * width + t + 1) * P]

            def two_banks(b):
                return [ps[:, b + h, 0:TH] for h in range(2)]

            def rms(norm, bank, tok_bank=None):
                pe.wait_ge(ssum_done, KT * (norm + 1))
                for h in range(2):
                    mm = pe.matmul(ps[:, bank + h, 0:TH], ones[:, :], ssum[:, h * TH:(h + 1) * TH], start=True, stop=True)
                if tok_bank is not None:
                    for g in range(2):
                        for tb in range(5 - g):
                            cols, c = tokens(tb, g), rtok_col(tb, g)
                            mm = pe.matmul(ps[0:(NSAMP if tb == 4 else P), tok_bank, c:c + 1], ssum[:, cols],
                                           ones[:, 0:1], start=True, stop=True)
                mm.then_inc(rms_ready, 1)

            def memory_keys_values():
                def memory_rms():
                    pe.wait_ge(ones_set, 1)
                    pe.wait_ge(m_sum, 1)
                    pe.matmul(ps[:, 6, 0:MEM], ones[:, :], msum[:, :], start=True, stop=True)
                    for tb in range(2):
                        mm = pe.matmul(ps[:, 7, tb:tb + 1], msum[:, tb * P:(tb + 1) * P], ones[:, 0:1], start=True,
                                       stop=True)
                    mm.then_inc(m_rms, 1)

                for layer in range(2):
                    def m_ready(kt, layer=layer):
                        pe.wait_ge(m_head, KT * layer + kt + 1)
                        pe.wait_ge(m_rest, KT * layer + kt + 1)
                    for part in range(2):
                        n = 2 * layer + part
                        chunk_ready(n)
                        for t in range(2):
                            unit = 2 * n + t
                            if unit >= 4:
                                pe.wait_ge(mkv_done, unit - 3)
                            if part == 0:
                                mm = product([ps[:, unit % 4, 0:MEM]], tile_of(wh, n % 2, t), tile_of(wl, n % 2, t),
                                             lambda kt: [mh[layer][:, kt, :]], lambda kt: [ml[layer][:, kt, :]], KT,
                                             m_ready if t == 0 else None)
                            else:
                                mm = product([ps[:, unit % 4, 0:MEM]], lambda kt: mh[layer][:, kt, t * P:(t + 1) * P],
                                             lambda kt: ml[layer][:, kt, t * P:(t + 1) * P],
                                             lambda kt: [wh[:, n % 2, kt * 256:(kt + 1) * 256]],
                                             lambda kt: [wl[:, n % 2, kt * 256:(kt + 1) * 256]], KT)
                            mm.then_inc(w_used if t else m_first, 1)
                            if unit == 0:
                                memory_rms()
                pe.wait_ge(mkv_done, 8)
                pe.wait_ge(m_sqrt, 2)

            def ffn(f):
                n, g, acc, norm = plan[f"ffn{f}"], FT * f, FFN_ACC[f], FFN_NORM[f]
                for h in range(2):
                    count = HALF_TILES[h]

                    def in_chunk(n_, slot, s, gates=None):
                        chunk_ready(n_)
                        for t in range(2):
                            mm = product(two_banks(4 * s + 2 * t), tile_of(wh, slot, t), tile_of(wl, slot, t),
                                         by_halves(xh), by_halves(xl), KT, gates if t == 0 else None)
                            if t == 0 and gates is not None:
                                if acc:
                                    pe.wait_ge(y_added, acc)
                                rms(norm, 4)
                        mm.then_inc(w_used, 1)

                    def x_ready(kt):
                        pe.wait_ge(x_head, KT * norm + kt + 1)
                        pe.wait_ge(x_rest, KT * norm + kt + 1)

                    if h == 0:
                        if acc:
                            pe.wait_ge(y_added, acc - 1)
                        in_chunk(n, n % 2, 0, x_ready)
                        pe.wait_ge(rms_read, norm + 1)
                        in_chunk(n + 1, (n + 1) % 2, 1)
                    else:
                        pe.wait_ge(y_added, acc - 1)
                        in_chunk(n, n % 2, 0)
                        pe.wait_ge(y_added, acc)
                        in_chunk(n + 1, (n + 1) % 2, 1)
                    with pe.Fori(1, count // 2) as i:
                        for b in range(2):
                            pe.wait_ge(up_ready, 2 * i + (g + b - 1))
                            in_chunk(2 * i + (n + b), (n + b) % 2, b)
                    n += count
                    g += count

                    def out_chunk(n_, slot, b, gates=None):
                        chunk_ready(n_)
                        product(two_banks(4 * b), tile_of(wh, slot, 0, 1), tile_of(wl, slot, 0, 1), by_halves(acth),
                                by_halves(actl), count, gates).then_inc(w_used, 1)

                    def hidden_ready(kt):
                        pe.wait_ge(act_head, g - count + kt + 1)
                        pe.wait_ge(act_rest, g - count + kt + 1)

                    pe.wait_ge(up_ready, g - 1)
                    out_chunk(n, n % 2, 0, hidden_ready)
                    pe.wait_ge(up_ready, g)
                    out_chunk(n + 1, (n + 1) % 2, 1)
                    with pe.Fori(1, KT // 2) as i:
                        for b in range(2):
                            pe.wait_ge(y_added, 2 * i + (acc + b - 1))
                            out_chunk(2 * i + (n + b), (n + b) % 2, b)
                    n += KT
                    acc += KT

            def tiles_in(M, first, last):
                norm, T0 = M["norm"], M["tile0"]

                def x_ready(kt):
                    pe.wait_ge(x_head, KT * norm + kt + 1)
                    pe.wait_ge(x_rest, KT * norm + kt + 1)

                for t in range(first, last + 1):
                    if t < last:
                        n = M["chunk"] + t // 2
                        if t % 2 == 0:
                            chunk_ready(n)
                        if t == 0:
                            pe.wait_ge(y_added, M["acc"] - 1)
                        if t == 2:
                            pe.wait_ge(tok_read, (norm + 2) // 3)
                        if t >= 3:
                            pe.wait_ge(raw_ready, T0 + t - 2)
                        done, _ = tile_done(M, t)
                        product(two_banks(2 * (t % 3)), tile_of(wh, n % 2, t % 2), tile_of(wl, n % 2, t % 2),
                                by_halves(xh), by_halves(xl), KT, x_ready if t == 0 else None).then_inc(done, 1)
                        if t == 0:
                            pe.wait_ge(y_added, M["acc"])
                            rms(norm, 6, 4)
                    if t > first and t - 1 in M["roped"]:
                        k = M["rope0"] + M["roped"].index(t - 1)
                        pe.wait_ge(raw_ready, T0 + t)
                        if k >= 1:
                            pe.wait_ge(sin_ready, k)
                        if t == 1:
                            pe.wait_ge(rms_read, norm + 1)
                        for h in range(2):
                            mm = pe.matmul(ps[:, 6 + h, 0:TH], rot[:, :], M["tiles"][t - 1][:, h * TH:(h + 1) * TH],
                                           start=True, stop=True)
                        mm.then_inc(rot_ready, 1)

            def ropes_before(M, t):
                return M["rope0"] + sum(i < t for i in M["roped"])

            def values_in(M):
                pe.wait_ge(raw_ready, M["tile0"] + M["ntiles"])
                for i, (g, tb) in enumerate(M["v_units"]):
                    n = M["chunk"] + M["ntiles"] // 2 + g
                    if tb == 0:
                        chunk_ready(n)
                    if i >= 3:
                        pe.wait_ge(v_done, M["v0"] + i - 2)
                    rows = NSAMP if tb == 4 else P
                    done, _ = v_block_done(M, i)
                    product([ps[0:rows, 2 * (i % 3), 0:256]], lambda kt: xh[:, kt, tokens(tb, g)],
                            lambda kt: xl[:, kt, tokens(tb, g)], lambda kt: [wh[:, n % 2, kt * 256:(kt + 1) * 256]],
                            lambda kt: [wl[:, n % 2, kt * 256:(kt + 1) * 256]], KT).then_inc(done, 1)
                pe.wait_ge(v_done, M["v0"] + len(M["v_units"]))
                pe.wait_ge(roped, ropes_before(M, M["ntiles"]))

            def scores(q, layer):
                if q["before"]:
                    pe.wait_ge(s_masked, q["before"]["u"] + 1)
                rows = slice(64 * q["half"], 64 * q["half"] + 64)
                if q["kind"] == "b":
                    for g in range(3):
                        every = slice(q["blk"], SEQ, 4)
                        keys = slice(0, SEQ) if g == 0 else every
                        at, w = q["s0"] + (0, SEQ, SEQ + P)[g], SEQ if g == 0 else P
                        mm = pe.matmul(psf[:, at:at + w], b_tiles[2 * g + q["tile"]][rows, every],
                                       b_tiles[6 + 2 * g + q["tile"]][rows, keys], start=True, stop=True)
                else:
                    if q["kind"] == "a":
                        queries, keys = a_tiles[6 + q["tile"]], a_tiles[12 + q["kv"] // 2][rows, 0:q["cols"]]
                    else:
                        queries, keys = a_tiles[mixers[layer]["mem_q"] + q["tile"]], memk[rows, layer, q["tile"], :]
                    mm = pe.matmul(psf[:, q["s0"]:q["s0"] + q["cols"]], queries[rows, q["blk"] * P:(q["blk"] + 1) * P],
                                   keys, start=True, stop=True)
                mm.then_inc(s_ready, 1)

            def turn(q):
                pe.wait_ge(p_ready, q["u"] + 1)
                for g, at, k in q["groups"]:
                    if g >= 2:
                        pe.wait_ge(pt_copied, g - 1)
                    for i in range(k):
                        mm = pe.matmul(ps[:, 4 + g % 2, i * P:(i + 1) * P],
                                       pbuf[:, q["s0"] + (at + i) * P:q["s0"] + (at + i + 1) * P],
                                       diag[:, q["u"] % 4, :], start=True, stop=True)
                    mm.then_inc(pt_ready, 1)

            def values_of(q, layer, tile):
                cols = slice(64 * q["kv"], 64 * q["kv"] + 64)
                if q["kind"] == "a":
                    return a_v[:, tile, cols]
                if q["kind"] == "b":
                    return b_v[:, 0, tile, cols] if tile < NBLK else b_v[:, tile - 3, q["blk"], cols]
                return memv[:, layer, tile, cols]

            def weigh(q, layer):
                if q["half"] == 0 and q["pair"] >= 2:
                    pe.wait_ge(o_stored, q["pair"] - 1)
                for g, at, k in q["groups"]:
                    pe.wait_ge(pt_copied, g + 1)
                    for i in range(k):
                        mm = pe.matmul(ps[64 * q["half"]:64 * q["half"] + 64, 6 + q["pair"] % 2, 0:P],
                                       values_of(q, layer, at + i), ptb[:, g % 2, i * P:(i + 1) * P],
                                       start=(at + i == 0), stop=(at + i == q["cols"] // P - 1))
                    mm.then_inc(pv_done, 1)

            def attend(layer, us):
                ahead = ATTEND_AHEAD[us[0]["kind"]]
                for q in us[:ahead]:
                    scores(q, layer)
                for k, q in enumerate(us):
                    if k + ahead < len(us):
                        scores(us[k + ahead], layer)
                    turn(q)
                    if k >= 1:
                        weigh(us[k - 1], layer)
                weigh(us[-1], layer)
                pe.wait_ge(o_stored, us[-1]["pair"] + 1)

            def indexer():
                pe.wait_ge(raw_ready, 6)
                pe.wait_ge(roped, 5)
                for tb in range(NBLK):
                    mm = pe.transpose(ps[:, 4, tb * 8:tb * 8 + 8], a_tiles[5][0:8, tb * P:(tb + 1) * P], ident[0:8, 0:8])
                mm = pe.matmul(ps[0:64, 5, 0:8], e8, a_tiles[5][0:8, SEQ:T], start=True, stop=True)
                mm.then_inc(iw_ready, 1)
                k = 0
                for blk in range(1, NBLK):
                    for h in range(8):
                        rows = slice(64 * (h % 2), 64 * (h % 2) + 64)
                        if k >= 4:
                            pe.wait_ge(ix_relu, k - 3)
                        pe.matmul(ps[:, k % 4, 0:(blk + 1) * P], a_tiles[h // 2][rows, blk * P:(blk + 1) * P],
                                  a_tiles[4][rows, 0:(blk + 1) * P], start=True, stop=True).then_inc(ix_ready, 1)
                        k += 1
                pe.wait_ge(ix_relu, k)
                pe.wait_ge(iw_done, 2)
                pe.wait_ge(q_placed, Q_PLACED["idx"])
                for pair in range(NSAMP // 2):
                    it = items[pair // 2]
                    pe.wait_ge(r_loaded[it["slot"]], it["loaded"])
                    stat, o = qmem[:, pair * 64:(pair + 1) * 64], pair % 2 * PAST
                    for j, keys in enumerate((slot(it["slot"])[:, o:o + 512], slot(it["slot"])[:, o + 512:o + PAST],
                                              a_tiles[4][:, SEQ:T])):
                        mm = pe.matmul(ps[0:64, j, 0:keys.shape[1]], stat, keys, start=(pair == 0), stop=(pair == 3))
                    if pair % 2:
                        mm.then_inc(r_used, 1)
                pe.wait_ge(six_relu, 1)
                for j, (at, w) in enumerate(((0, 512), (512, 512), (PAST, NSAMP))):
                    mm = pe.matmul(ps[0:8, 4 + j, 0:w], iws[:, :], work[0:64, at:at + w], start=True, stop=True)
                mm.then_inc(six_sum, 1)
                pe.wait_ge(six_done, 3)

            def row_scores(k):
                kind, layer = ROW_KIND[k], ROW_LAYER[k]
                rows, (per, kw, vw) = nrows(kind), ITEMS[kind]
                pe.wait_ge(q_placed, Q_PLACED[k])
                q_at = qmem if kind == "mem" else qblk
                its = [it for it in items if it["kind"] == kind and it["layer"] == layer]
                for it in [it for it in its if it["what"] == "key"]:
                    pe.wait_ge(r_loaded[it["slot"]], it["loaded"])
                    for b in range(it["first"], it["first"] + per):
                        keys = slot(it["slot"])[:, (b - it["first"]) * kw:(b - it["first"] + 1) * kw]
                        for p in range(2):
                            one = b == 0 and p == 0
                            end = b == NSAMP - 1 and p == 1

                            def stat(g=0):
                                o = ((2 * g + p) * NSAMP + b) * rows
                                return q_at[:, o:o + rows]
                            if kind == "a":
                                paged = keys.rearrange("q (g p c) -> q g p c", g=NPAGE, p=2)
                                for j in range(2):
                                    pe.matmul(ps[0:rows, j, :], stat(), paged[:, 4 * j:4 * j + 4, p, :], start=one,
                                              stop=False)
                                mm = pe.matmul(ps[0:rows, 2, 0:NSAMP], stat(), a_tiles[12 + p][:, SEQ:T], start=one,
                                               stop=False)
                            elif kind == "mem":
                                mm = pe.matmul(ps[0:rows, 3, 0:MEM], stat(), keys[:, p * MEM:(p + 1) * MEM], start=one,
                                               stop=end)
                            else:
                                at = 0
                                for g, w in enumerate(KEYS_B):
                                    pe.matmul(ps[0:rows, 0, at:at + w], stat(g),
                                              keys[:, 2 * at + p * w:2 * at + (p + 1) * w], start=one and g == 0,
                                              stop=False, skip_group_check=True)
                                    at += w
                                for g in range(3):
                                    mm = pe.matmul(ps[0:rows, 0, 320 + NSAMP * g:328 + NSAMP * g], stat(g),
                                                   b_tiles[6 + 2 * g + p][:, SEQ:T], start=False, stop=False,
                                                   skip_group_check=True)
                    mm.then_inc(r_used, 1)
                if kind == "a":
                    pe.wait_ge(mask_ready, 4)
                    for j, (at, w) in enumerate(((0, 512), (512, 512), (PAST, NSAMP))):
                        mm = pe.matmul(ps[0:rows, j, 0:w], e96, scs[0:8, at:at + w], start=False, stop=True)
                    mm.then_inc(row_ready, 1)
                elif kind == "b":
                    pe.matmul(ps[0:rows, 0, 320:COLS_B], ident[0:rows, 0:rows], offb, start=False, stop=True,
                              skip_group_check=True).then_inc(row_ready, 1)

            def row_turn(k):
                kind, rows = ROW_KIND[k], nrows(ROW_KIND[k])
                pe.wait_ge(row_norm, k + 1)
                for i, (at, w) in enumerate(row_tiles(kind)):
                    bank = 6 if kind == "mem" else 4 + i // 5
                    mm = pe.transpose(ps[0:w, bank, (i % 5) * rows:(i % 5 + 1) * rows], rowp[k % 2][0:rows, at:at + w],
                                      ident[0:rows, 0:rows])
                mm.then_inc(rowt_ready, 1)

            def row_weigh(k):
                kind, nh = ROW_KIND[k], nrows(ROW_KIND[k]) // NSAMP
                per, _, vw = ITEMS[kind]
                its = [it for it in items if (it["kind"], it["what"], it["layer"]) == (kind, "value", ROW_LAYER[k])]
                pe.wait_ge(rowt_copied, k + 1)
                if kind != "mem":
                    rows, news = nrows(kind), [i for i, (_, w) in enumerate(row_tiles(kind)) if w == NSAMP]
                    for p in range(2):
                        for i in news:
                            v = a_vs if kind == "a" else b_vs[:, i - len(KEYS_B), :]
                            mm = pe.matmul(ps[:, 6 + p, 0:rows], v[:, p * P:(p + 1) * P], rowt[1][0:NSAMP, i, 0:rows],
                                           start=(i == news[0]), stop=(i == news[-1]))
                    mm.then_inc(new_ready, 1)
                olds = [(i, w) for i, (_, w) in enumerate(row_tiles(kind)) if w > NSAMP]
                for it in its:
                    pe.wait_ge(r_loaded[it["slot"]], it["loaded"])
                    for b in range(it["first"], it["first"] + per):
                        out, cols = psf[OUT_AT[k % 2]:OUT_AT[k % 2] + nh, b * 256:(b + 1) * 256], slice(b * nh, (b + 1) * nh)
                        for n, (i, w) in enumerate(olds):
                            o = (b - it["first"]) * vw + i * 256
                            mm = pe.matmul(out, rowt[k % 2][0:w, i, cols], slot(it["slot"])[0:w, o:o + 256],
                                           start=(n == 0), stop=(n == len(olds) - 1))
                    mm.then_inc(r_used, 1)

            def row_finish(k):
                nh, o, bank = nrows(ROW_KIND[k]) // NSAMP, OUT_AT[k % 2], 4 if ROW_KIND[k] == "mem" else 6
                pe.wait_ge(rowv_copied[k % 2], 2 * (k // 2) + 2)
                if ROW_KIND[k] != "mem":
                    pe.wait_ge(new_copied, k // 2 + 1)
                for b in range(NSAMP):
                    for p in range(2):
                        mm = pe.transpose(ps[:, bank + p, b * nh:(b + 1) * nh],
                                          rowo[o:o + nh, b * 256 + p * P:b * 256 + (p + 1) * P], ident[o:o + nh, o:o + nh])
                mm.then_inc(rowo_ready, 1)

            def sample_rows(layer):
                ks = (2 * layer, 2 * layer + 1)
                row_scores(ks[0])
                row_scores(ks[1])
                for k in ks:
                    row_turn(k)
                    row_weigh(k)
                for k in ks:
                    row_finish(k)
                pe.wait_ge(rowo_stored, 2 * layer + 2)

            def tiles_out(M):
                per, acc, nk = out_tiles_per_chunk(M), M["acc"], M["out_kt"]

                pe.wait_ge(ot_head, M["ot0"] + nk + 1)
                pe.wait_ge(ot_rest, M["ot0"] + nk + 1)
                for m in range(KT):
                    n = M["out_chunk"] + m // per
                    if m % per == 0:
                        chunk_ready(n)
                    if m >= 2:
                        pe.wait_ge(y_added, acc + m - 1)
                    done, _ = out_done(M, m)
                    product(two_banks(4 * (m % 2)), tile_of(wh, n % 2, m % per, per), tile_of(wl, n % 2, m % per, per),
                            by_halves(acth), by_halves(actl), nk).then_inc(done, 1)

            pe.wait_ge(const_loaded, 16 * 4)
            memory_keys_values()
            ffn(0)
            A, B = mixers
            pe.wait_ge(rope_loaded, 16 * 4)
            tiles_in(A, 0, 6)
            indexer()
            tiles_in(A, 6, 16)
            values_in(A)
            attend(0, units[0])
            sample_rows(0)
            tiles_out(A)
            ffn(1)
            ffn(2)
            tiles_in(B, 0, 14)
            values_in(B)
            attend(1, units[1][:16])
            attend(1, units[1][16:])
            sample_rows(1)
            tiles_out(B)
            ffn(3)
            pe.wait_ge(y_added, 80)
            rms(6, 0)

        @block.scalar
        def _(act):
            def split(n, i=None):
                more = 0 if i is None else i
                act.wait_ge(w_loaded[n % 2], 16 * more + 16 * (n // 2 + 1))
                if n >= 2:
                    act.wait_ge(w_used, 2 * more + (n - 1))
                act.activation(wh[:, n % 2, :], raw[:, n % 2, :], ACT.Copy).then_inc(w_head, 1)

            copies = [0]

            def copy_state(count):
                for _ in range(count):
                    if copies[0] == 3 * NSAMP:
                        return
                    which, b = copies[0] % 3, copies[0] // 3
                    act.dma_start(outs[f"state{which}"][b], ins[f"state{which}"][b]).then_inc(copied, 16)
                    copies[0] += 1

            def prepare(norm, m, acc=None, i=None, last=False):
                at = m if i is None else 2 * i + m
                more = 0 if i is None else 2 * i
                if acc is not None:
                    act.wait_ge(y_added, more + (acc + m + 1))
                if norm > 0 or m >= 2:
                    act.wait_ge(ssum_done, more + (KT * norm + m - 1))
                tile = y[:, m, :] if i is None else y[:, bass.ds(at, 1), :].rearrange("p a t -> p (a t)")
                act.activation(tu[:, m % 2, :], tile, ACT.Square).then_inc(sq_ready, 1)
                if not last:
                    gain = gains[:, norm, m:m + 1] if i is None else gains[:, norm, bass.ds(at, 1)]
                    to = xh[:, m, :] if i is None else xh[:, bass.ds(at, 1), :].rearrange("p a t -> p (a t)")
                    act.activation(to, tile, ACT.Identity, scale=gain).then_inc(x_head, 1)

            def root(norm, bank, tok_bank=None):
                act.wait_ge(rms_ready, norm + 1)
                act.activation(halves(rstd[:, :]), bank2(bank), ACT.Sqrt, bias=epsb[:, 0:1], scale=1.0 / D)\
                   .then_inc(rms_read, 1)
                if tok_bank is not None:
                    for r, cols in ((P, slice(0, 4)), (NSAMP, slice(4, 5)), (P, slice(5, 9))):
                        a = act.activation(rtok[0:r, cols], ps[0:r, tok_bank, cols], ACT.Sqrt, bias=epsb[0:r, 0:1],
                                           scale=1.0 / D)
                    a.then_inc(tok_read, 1)

            def memory_keys_values():
                def heads(layer):
                    for kt in range(KT):
                        act.activation(mh[layer][:, kt, :], mraw[:, kt, :], ACT.Identity,
                                       scale=gains[:, 7 + layer, kt:kt + 1]).then_inc(m_head, 1)
                split(0)
                act.wait_ge(mem_loaded, 16)
                act.wait_ge(const_loaded, 64)
                heads(0)
                act.activation(msq[:, :, :], mraw[:, :, :], ACT.Square).then_inc(m_sq, 1)
                split(1)
                heads(1)
                act.wait_ge(m_rms, 1)
                act.activation(mrstd[:, :], ps[:, 6, 0:MEM], ACT.Sqrt, bias=epsb[:, 0:1], scale=1.0 / D).then_inc(m_sqrt, 1)
                act.activation(mrtok[:, :], ps[:, 7, 0:2], ACT.Sqrt, bias=epsb[:, 0:1], scale=1.0 / D).then_inc(m_sqrt, 1)
                split(2)
                act.wait_ge(y_loaded, 16)
                for m in range(4):
                    prepare(0, m)
                split(3)
                for m in range(4, KT):
                    prepare(0, m)
                split(4)
                split(5)
                act.wait_ge(mkv_done, 8)
                act.dma_start(outs["memk"], memk[:, :, :, :]).then_inc(out_written, 16)
                act.dma_start(outs["memv"], memv[:, :, :, :]).then_inc(out_written, 16)

            def ffn(f):
                n, g, acc, norm = plan[f"ffn{f}"], FT * f, FFN_ACC[f], FFN_NORM[f]
                for h in range(2):
                    count = HALF_TILES[h]

                    def in_tile(b, i):
                        act.wait_ge(gate_ready, 2 * i + (g + b + 1))
                        act.activation(tg[:, b, :], tg[:, b, :], ACT.Silu).then_inc(silu_ready, 1)
                        act.wait_ge(hid_ready, 2 * i + (g + b + 1))
                        act.activation(acth[:, bass.ds(2 * i + b, 1), :].rearrange("p a t -> p (a t)"), tg[:, b, :],
                                       ACT.Copy).then_inc(act_head, 1)
                        split(n + b + 2, i)
                    if h == 0:
                        root(norm, 4)
                    copy_state(2)
                    with act.Fori(0, count // 2) as i:
                        for b in range(2):
                            in_tile(b, i)
                    n += count
                    g += count
                    copy_state(2)
                    if h == 0:
                        with act.Fori(0, KT // 2) as i:
                            for b in range(2):
                                split(n + b + 2, i)
                    elif f < 3:
                        with act.Fori(0, KT // 2) as i:
                            for b in range(2):
                                prepare(norm_after(f), b, acc, i)
                                split(n + b + 2, i)
                    else:
                        for m in range(KT):
                            prepare(6, m, acc, last=True)
                            if m < KT - 2:
                                split(n + m + 2)
                    n += KT
                    acc += KT

            def tiles_in(M, first, last):
                for t in range(first, last):
                    if t == 0:
                        root(M["norm"], 6, 4)
                    if t % 2 == 1 and M["chunk"] + t // 2 + 2 < M["out_chunk"]:
                        split(M["chunk"] + t // 2 + 2)

            def values_in(M):
                for i, (g, tb) in enumerate(M["v_units"]):
                    done, count = v_block_done(M, i)
                    act.wait_ge(done, count)
                    act.wait_ge(rtok_ready, (M["norm"] + 2) // 3)
                    rows, col = NSAMP if tb == 4 else P, rtok_col(tb, g)
                    to = (a_vs[:, :] if tb == 4 else a_v[:, tb, :]) if M["layer"] == 0 else \
                        (b_vs[:, g, :] if tb == 4 else b_v[:, g, tb, :])
                    act.activation(to, ps[0:rows, 2 * (i % 3), 0:256], ACT.Copy, scale=rtok[0:rows, col:col + 1])\
                       .then_inc(v_done, 1)
                    if tb == 4 and M["chunk"] + M["ntiles"] // 2 + g + 2 < M["out_chunk"]:
                        split(M["chunk"] + M["ntiles"] // 2 + g + 2)
                act.wait_ge(v_done, M["v0"] + len(M["v_units"]))
                act.wait_ge(roped, M["rope0"] + len(M["roped"]))
                if M["layer"] == 0:
                    stores = ((outs["kidx"], a_tiles[4][0:64, :]), (outs["k_a"], tiles[:, 12:14, :]),
                              (outs["v_a"], a_v[:, :, :]), (outs["vs_a"], a_vs[:, :]))
                else:
                    stores = ((outs["k_b"], tiles[:, 6:12, :]), (outs["v_b"], b_v[:, :, :, :]),
                              (outs["vs_b"], b_vs[:, :, :]))
                for to, src in stores:
                    act.dma_start(to, src).then_inc(out_written, 16)

            def exponent(q):
                act.wait_ge(nmax_ready, q["u"] + 1)
                p = pbuf[:, q["s0"]:q["s0"] + q["cols"]]
                act.activation(p, p, ACT.Exp, bias=stats[:, 1, q["u"] % 4:q["u"] % 4 + 1], scale=SCALE,
                               accum_out=stats[:, 2, q["u"] % 4:q["u"] % 4 + 1]).then_inc(exp_ready, 1)

            def copy_turned(q):
                for g, at, k in q["groups"]:
                    act.wait_ge(pt_ready, g + 1)
                    if g >= 2:
                        act.wait_ge(pv_done, g - 1)
                    act.activation(ptb[:, g % 2, 0:k * P], ps[:, 4 + g % 2, 0:k * P], ACT.Copy).then_inc(pt_copied, 1)

            def store(q):
                if q["half"] == 1:
                    act.wait_ge(pv_done, q["groups"][-1][0] + 1)
                    b = q["blk"]
                    cols = slice(b, SEQ, 4) if q["kind"] == "b" else slice(b * P, (b + 1) * P)
                    act.activation(ot[:, q["out"], cols], ps[:, 6 + q["pair"] % 2, 0:P], ACT.Copy).then_inc(o_stored, 1)

            def attend(us):
                ahead = ATTEND_AHEAD[us[0]["kind"]]
                for q in us[:ahead - 1]:
                    exponent(q)
                for k, q in enumerate(us):
                    if k + ahead - 1 < len(us):
                        exponent(us[k + ahead - 1])
                    copy_turned(q)
                    if k >= 2:
                        store(us[k - 2])
                store(us[-2])
                store(us[-1])

            def indexer():
                act.wait_ge(iw_ready, 1)
                act.activation(iwt[:, :, :].rearrange("p a b -> p (a b)"), ps[:, 4, 0:32], ACT.Copy, scale=IDX_SCALE)\
                   .then_inc(iw_done, 1)
                k = 0
                for blk in range(1, NBLK):
                    for h in range(8):
                        act.wait_ge(ix_ready, k + 1)
                        if k >= 2:
                            act.wait_ge(ix_added, k - 1)
                        act.activation(tg[:, k % 2, 0:(blk + 1) * P], ps[:, k % 4, 0:(blk + 1) * P], ACT.Relu)\
                           .then_inc(ix_relu, 1)
                        k += 1
                act.wait_ge(r_used, 2)
                act.activation(work[0:64, :], psf[0:64, 0:COLS_A], ACT.Relu).then_inc(six_relu, 1)

            def outputs_head(k):
                M = mixers[ROW_LAYER[k]]
                act.wait_ge(out_written, 16 * (2 + 4 if M["layer"] == 0 else 2 + 4 + 3))
                act.wait_ge(o_stored, units[M["layer"]][-1]["pair"] + 1)
                for kt in range(M["out_kt"]):
                    act.activation(acth[:, kt, 0:SEQ], ot[:, kt, 0:SEQ], ACT.Copy).then_inc(ot_head, 1)

            def weights_head(k):
                M = mixers[ROW_LAYER[k]]
                for c in range(2):
                    act.wait_ge(r_used, last_in_place(k, M["out_chunk"] + c) + 1)
                    split(M["out_chunk"] + c)

            def pages_of(rs):
                for it in items:
                    if it["r"] in rs:
                        act.wait_ge(r_used, it["after"] + 1)
                        load_pages(act, it)

            def row_exponent(k):
                kind = ROW_KIND[k]
                rows, cols, at = nrows(kind), row_cols(kind), 1536 if kind == "mem" else 0
                act.wait_ge(row_max, k + 1)
                act.activation(rowp[k % 2][0:rows, 0:cols], psf[0:rows, at:at + cols], ACT.Exp,
                               bias=rstat[0:rows, k % 2, 1:2], scale=SCALE, accum_out=rstat[0:rows, k % 2, 2:3])\
                   .then_inc(row_exp, 1)

            def row_copy_turned(k):
                kind, rows = ROW_KIND[k], nrows(ROW_KIND[k])
                act.wait_ge(rowt_ready, k + 1)
                n = len(row_tiles(kind))
                parts = [(i, i + 1) for i in range(n) if row_tiles(kind)[i][1] < P]
                whole = sum(w == P for _, w in row_tiles(kind))
                parts = [(0, min(whole, 5))] + ([(5, whole)] if whole > 5 else []) + parts
                for a, b in parts:
                    w, bank = row_tiles(kind)[a][1], 6 if kind == "mem" else 4 + a // 5
                    last = act.activation(rowt[k % 2][0:w, a:b, 0:rows],
                                          ps[0:w, bank, (a % 5) * rows:(a % 5 + b - a) * rows]
                                          .rearrange("p (i r) -> p i r", r=rows), ACT.Copy)
                last.then_inc(rowt_copied, 1)

            def row_copy_out(k):
                nh, o = nrows(ROW_KIND[k]) // NSAMP, OUT_AT[k % 2]
                act.wait_ge(r_used, LAST_VALUES[k] + 1)
                act.activation(rowo[o:o + nh, 0:1024], psf[o:o + nh, 0:1024], ACT.Copy).then_inc(rowv_copied[k % 2], 1)

            def sample_rows(layer):
                pages = BY_SCALAR if layer == 0 else []
                k = 2 * layer
                pages_of(pages[:2])
                outputs_head(k)
                row_exponent(k)
                row_copy_turned(k)
                row_exponent(k + 1)
                row_copy_turned(k + 1)
                rows = nrows(ROW_KIND[k + 1])
                act.wait_ge(new_ready, layer + 1)
                act.activation(rown[:, :, 0:rows], ps[:, 6:8, 0:rows], ACT.Copy).then_inc(new_copied, 1)
                pages_of(pages[2:])
                row_copy_out(k)
                weights_head(k)
                row_copy_out(k + 1)

            def tiles_out(M):
                act.wait_ge(rowo_stored, 2 * M["layer"] + 2)
                act.activation(acth[:, 0:M["out_kt"], SEQ:T], ot[:, 0:M["out_kt"], SEQ:T], ACT.Copy).then_inc(ot_head, 1)
                for m in range(KT):
                    prepare(M["norm"] + 1, m, M["acc"])
                    if (m + 1) % out_tiles_per_chunk(M) == 0:
                        split(M["out_chunk"] + m // out_tiles_per_chunk(M) + 2)

            def norm_after(f):
                return [1, 3, 4, 6][f]

            memory_keys_values()
            ffn(0)
            A, B = mixers
            tiles_in(A, 0, 6)
            indexer()
            tiles_in(A, 6, 16)
            values_in(A)
            attend(units[0])
            sample_rows(0)
            tiles_out(A)
            ffn(1)
            ffn(2)
            tiles_in(B, 0, 14)
            values_in(B)
            attend(units[1][:16])
            attend(units[1][16:])
            sample_rows(1)
            tiles_out(B)
            ffn(3)
            root(6, 0)

        @block.vector
        def _(dve):
            def split(n, i=None):
                more = 0 if i is None else 2 * i
                dve.wait_ge(w_head, more + (n + 1))
                dve.tensor_tensor(wl[:, n % 2, :], raw[:, n % 2, :], wh[:, n % 2, :].bitcast(F32), ALU.subtract)\
                   .then_inc(w_rest, 1)

            def prepare(norm, m, i=None):
                more = 0 if i is None else 2 * i
                dve.wait_ge(x_head, more + (KT * norm + m + 1))
                if i is None:
                    tile, gain, head, rest = y[:, m, :], gains[:, norm, m:m + 1], xh[:, m, :], xl[:, m, :]
                else:
                    at = bass.ds(2 * i + m, 1)
                    tile, head, rest = (v[:, at, :].rearrange("p a t -> p (a t)") for v in (y, xh, xl))
                    gain = gains[:, norm, at]
                dve.scalar_tensor_tensor(rest, tile, gain, head.bitcast(F32), ALU.mult, ALU.subtract)\
                   .then_inc(x_rest, 1)

            def invert(norm, tok=False):
                dve.wait_ge(rms_read, norm + 1)
                dve.reciprocal(rstd[:, :], rstd[:, :]).then_inc(rstd_ready, 1)
                if tok:
                    dve.wait_ge(tok_read, (norm + 2) // 3)
                    for r, cols in ((P, slice(0, 4)), (NSAMP, slice(4, 5)), (P, slice(5, 9))):
                        d = dve.reciprocal(rtok[0:r, cols], rtok[0:r, cols])
                    d.then_inc(rtok_ready, 1)

            def add_out(scale, m, acc, done, count, i=None):
                more = 0 if i is None else 2 * i
                dve.wait_ge(done, more + count)
                if acc + m > 0:
                    dve.wait_ge(y_added, more + (acc + m))
                tile = y[:, m, :] if i is None else y[:, bass.ds(2 * i + m, 1), :].rearrange("p a t -> p (a t)")
                dve.scalar_tensor_tensor(halves(tile), bank2(4 * (m % 2)), scale, halves(tile), ALU.mult, ALU.add)\
                   .then_inc(y_added, 1)

            def memory_keys_values():
                dve.memset(ones[:, :], 1.0).then_inc(ones_set, 1)
                def rests(layer):
                    for kt in range(KT):
                        dve.wait_ge(m_head, KT * layer + kt + 1)
                        dve.scalar_tensor_tensor(ml[layer][:, kt, :], mraw[:, kt, :], gains[:, 7 + layer, kt:kt + 1],
                                                 mh[layer][:, kt, :].bitcast(F32), ALU.mult, ALU.subtract)\
                           .then_inc(m_rest, 1)

                def take(n):
                    layer, part = n // 2, n % 2
                    for t in range(2):
                        dve.wait_ge(w_used if t else m_first, n + 1)
                        bank = ps[:, (2 * n + t) % 4, 0:MEM]
                        if part == 0:
                            dve.tensor_tensor(memk[:, layer, t, :], bank, mrstd[:, :], ALU.mult).then_inc(mkv_done, 1)
                        else:
                            dve.tensor_scalar(memv[:, layer, t, :], bank, mrtok[:, t:t + 1], None, ALU.mult)\
                               .then_inc(mkv_done, 1)
                split(0)
                dve.wait_ge(const_loaded, 16 * 4)
                dve.wait_ge(mem_loaded, 16)
                rests(0)
                dve.wait_ge(m_sq, 1)
                dve.tensor_reduce(msum[:, :], msq[:, :, :].rearrange("p k t -> p t k"), AX_X, ALU.add).then_inc(m_sum, 1)
                split(1)
                dve.wait_ge(m_sum, 1)
                rests(1)
                dve.wait_ge(m_sqrt, 2)
                dve.reciprocal(mrstd[:, :], mrstd[:, :]).then_inc(m_rstd, 1)
                dve.reciprocal(mrtok[:, :], mrtok[:, :]).then_inc(m_rstd, 1)
                dve.wait_ge(m_rstd, 2)
                take(0)
                split(2)
                for m in range(4):
                    prepare(0, m)
                take(1)
                split(3)
                for m in range(4, KT):
                    prepare(0, m)
                take(2)
                split(4)
                take(3)
                split(5)

            def ffn(f):
                n, g, acc, norm = plan[f"ffn{f}"], FT * f, FFN_ACC[f], FFN_NORM[f]
                for h in range(2):
                    count = HALF_TILES[h]

                    def in_tile(b, i, first=False):
                        more = 2 * i
                        dve.wait_ge(w_used, more + (n + b + 1))
                        if not first:
                            dve.wait_ge(act_rest, more + (g + b - 1))
                            dve.wait_ge(hid_ready, more + (g + b - 1))
                        dve.tensor_tensor(halves(tg[:, b, :]), bank2(4 * b), halves(rstd[:, :]), ALU.mult)\
                           .then_inc(gate_ready, 1)
                        dve.tensor_tensor(halves(tu[:, b, :]), bank2(4 * b + 2), halves(rstd[:, :]), ALU.mult)\
                           .then_inc(up_ready, 1)
                        dve.wait_ge(silu_ready, more + (g + b + 1))
                        dve.wait_ge(up_ready, more + (g + b + 1))
                        dve.tensor_tensor(tg[:, b, :], tg[:, b, :], tu[:, b, :], ALU.mult).then_inc(hid_ready, 1)
                        split(n + b + 2, i)

                    start = 0
                    if h == 0:
                        invert(norm)
                        dve.wait_ge(rstd_ready, [1, 3, 4, 6][f])
                        for b in range(2):
                            in_tile(b, 0, first=(f == 0))
                        start = 1
                    with dve.Fori(start, count // 2) as i:
                        for b in range(2):
                            in_tile(b, i)
                    n += count
                    g += count
                    if h == 0 or f < 3:
                        def out_tile(b, i):
                            add_out(0.5, b, acc, w_used, n + b + 1, i)
                            if h == 1:
                                prepare([1, 3, 4][f], b, i)
                            split(n + b + 2, i)
                        if acc == 0:
                            out_tile(0, 0)
                            out_tile(1, 0)
                        with dve.Fori(1 if acc == 0 else 0, KT // 2) as i:
                            for b in range(2):
                                out_tile(b, i)
                    else:
                        for m in range(KT):
                            add_out(0.5, m, acc, w_used, n + m + 1)
                            if m < KT - 2:
                                split(n + m + 2)
                    n += KT
                    acc += KT

            def tiles_in(M, first, last):
                def rotated(t):
                    k = M["rope0"] + M["roped"].index(t)
                    dve.wait_ge(rot_ready, k + 1)
                    if k >= 2:
                        dve.wait_ge(roped, k - 1)
                    dve.tensor_tensor(halves(tg[:, k % 2, :]), bank2(6), halves(sinf[:, :]), ALU.mult)\
                       .then_inc(sin_ready, 1)

                for t in range(first, last + 1):
                    if t == 0:
                        invert(M["norm"], True)
                        dve.wait_ge(rstd_ready, M["norm"] + 1)
                    if t < last:
                        done, count = tile_done(M, t)
                        dve.wait_ge(done, count)
                        dve.tensor_tensor(halves(M["tiles"][t]), bank2(2 * (t % 3)), halves(rstd[:, :]), ALU.mult)\
                           .then_inc(raw_ready, 1)
                    if t > first and t - 1 in M["roped"]:
                        rotated(t - 1)
                    if t < last and t % 2 == 1 and M["chunk"] + t // 2 + 2 < M["out_chunk"]:
                        split(M["chunk"] + t // 2 + 2)
                    if M["layer"] == 0 and t > 6:
                        search_steps(6)

            def values_in(M):
                for i, (g, tb) in enumerate(M["v_units"]):
                    if tb == 4 and M["chunk"] + M["ntiles"] // 2 + g + 2 < M["out_chunk"]:
                        split(M["chunk"] + M["ntiles"] // 2 + g + 2)
                if M["layer"] == 0:
                    search_steps(12)

            def spread(buf, parts, at, step):
                return buf[parts, at:at + (NSAMP - 1) * step + 1:step]

            def place_rows(M, ks):
                dve.wait_ge(raw_ready, M["tile0"] + M["ntiles"])
                dve.wait_ge(roped, M["rope0"] + len(M["roped"]))
                for k in ks:
                    place_block(k)

            def place_block(k):
                kind, layer = ROW_KIND[k], ROW_LAYER[k]
                dve.wait_ge(q_zeroed, Q_ZEROED[k])
                lo, hi = slice(0, 64), slice(64, P)
                if kind == "a":
                    for t, (ha, hb) in enumerate(PAIRS_A):
                        for parts, h in ((lo, ha), (hi, hb)):
                            dve.tensor_copy(spread(qblk, parts, (t // 3) * NSAMP * ROWS_A + h, ROWS_A + 12),
                                            a_tiles[6 + t][parts, SEQ:T]).then_inc(q_placed, 1)
                else:
                    to = qmem if kind == "mem" else qblk
                    for t in range(2 if kind == "mem" else 6):
                        src = (a_tiles[mixers[layer]["mem_q"] + t]) if kind == "mem" else b_tiles[t]
                        for half, parts in enumerate((lo, hi)):
                            dve.tensor_copy(spread(to, parts, t * NSAMP * ROWS_4 + 2 * (t % 2) + half, ROWS_4 + 4),
                                            src[parts, SEQ:T]).then_inc(q_placed, 1)

            def attend(us, extra=None):
                def masked(q):
                    u, col = q["u"], q["u"] % 4
                    dve.wait_ge(s_ready, u + 1)
                    if q["before"]:
                        dve.wait_ge(pt_ready, q["before"]["groups"][-1][0] + 1)
                    if u >= 4:
                        dve.wait_ge(p_ready, u - 3)
                    w, s0 = q["cols"], q["s0"]
                    out, src = pbuf[:, s0:s0 + w], psf[:, s0:s0 + w]
                    if q["kind"] == "mem":
                        dve.tensor_scalar(out, src, 1.0, TAKEN, ALU.mult, ALU.max, accum_out=stats[:, 0, col:col + 1])\
                           .then_inc(s_masked, 1)
                    elif q["kind"] == "a" and q["blk"] == 0:
                        dve.tensor_tensor_reduce(out, src, causal[:, :], 1.0, NEG, ALU.add, ALU.max,
                                                 stats[:, 0, col:col + 1]).then_inc(s_masked, 1)
                    else:
                        if q["kind"] == "a":
                            search_steps(2 * (TOPK_PROMPT // 8 + 1) * q["blk"] - searched[0])
                            dve.wait_ge(mask_ready, q["blk"])
                            mask = a_maskb[:, SC0[q["blk"]]:SC0[q["blk"]] + w]
                        else:
                            dve.wait_ge(bmask_loaded[q["blk"] % 2], 16 * (q["blk"] // 2 + 1))
                            mask = b_mask[q["blk"] % 2]
                        dve.tensor_tensor_reduce(out, src, mask, 1.0, NEG, ALU.add, ALU.max,
                                                 stats[:, 0, col:col + 1]).then_inc(s_masked, 1)
                    dve.wait_ge(s_masked, u + 1)
                    dve.tensor_scalar(stats[:, 1, col:col + 1], stats[:, 0, col:col + 1], -SCALE, None, ALU.mult)\
                       .then_inc(nmax_ready, 1)

                def inverse(q):
                    col = q["u"] % 4
                    dve.wait_ge(exp_ready, q["u"] + 1)
                    dve.reciprocal(stats[:, 3, col:col + 1], stats[:, 2, col:col + 1]).then_inc(den_ready, 1)

                ahead = ATTEND_AHEAD[us[0]["kind"]]
                for q in us[:ahead]:
                    masked(q)
                for q in us[:ahead - 1]:
                    inverse(q)
                for k in range(len(us)):
                    if k + ahead - 1 < len(us):
                        inverse(us[k + ahead - 1])
                    if k + ahead < len(us):
                        masked(us[k + ahead])
                    if extra:
                        extra(k)

            chained = [0]

            def chain(ins):
                ins.then_inc(chain_done, 1)
                chained[0] += 1

            def settle():
                dve.wait_ge(chain_done, chained[0])

            def search_operands(which):
                if which < 4:
                    cols = slice(SC0[which], SC0[which] + (which + 1) * P)
                    return (a_sc[:, cols], tkw[:, 0:(which + 1) * P], a_maskb[:, cols], TOPK_PROMPT,
                            tk[:, which, :])
                return (scs[0:8, 0:PAST + 1], work[0:8, 0:PAST + 1], a_sc[0:8, 0:PAST + 1], TOPK_SAMPLE, tk[0:8, 0, :])

            def find(which, r, half):
                sc, wk, _, k, found = search_operands(which)
                if half == 0:
                    settle()
                    chain(dve.max(found[:, 0:8], sc if r == 0 else wk))
                elif r < k // 8 - 1:
                    settle()
                    chain(dve.match_replace(wk, found[:, 0:8], sc if r == 0 else wk, TAKEN))

            def select(which):
                sc, wk, out, k, found = search_operands(which)
                least, count, need = found[:, 7:8], found[:, 8:9], found[:, 9:10]
                settle()
                chain(dve.tensor_scalar(out, sc, least, 0.0, ALU.is_gt, ALU.add, accum_out=count))
                settle()
                chain(dve.tensor_scalar(need, count, -1.0, float(k), ALU.mult, ALU.add))
                chain(dve.tensor_scalar(sc, sc, least, None, ALU.is_equal))
                settle()
                chain(dve.tensor_tensor_scan(wk, sc, sc, 0.0, ALU.add, ALU.max))
                settle()
                chain(dve.scalar_tensor_tensor(wk, wk, need, sc, ALU.is_le, ALU.mult))
                settle()
                chain(dve.tensor_tensor(out, out, wk, ALU.add))
                settle()
                if which < 4:
                    dve.tensor_scalar(out, out, -1.0, -NEG, ALU.add, ALU.mult).then_inc(mask_ready, 1)
                else:
                    chain(dve.tensor_scalar(sc, out, -1.0, -NEG, ALU.add, ALU.mult))
                    settle()
                    chain(dve.tensor_copy(found[:, 0:1], scs[0:8, PAST:PAST + 1]))
                    settle()
                    dve.tensor_scalar(scs[0:8, PAST:COLS_A], offm, found[:, 0:1], None, ALU.add)\
                       .then_inc(mask_ready, 1)

            searched = [0]

            def search_steps(count=SEARCH_STEPS):
                per = 2 * (TOPK_PROMPT // 8 + 1)
                end = min(searched[0] + max(count, 0), SEARCH_STEPS)
                for at in range(searched[0], end):
                    which, step = (1 + at // per, at % per) if at < 3 * per else (4, at - 3 * per)
                    if step // 2 < (TOPK_PROMPT if which < 4 else TOPK_SAMPLE) // 8:
                        find(which, step // 2, step % 2)
                    elif step % 2:
                        select(which)
                searched[0] = end

            def indexer():
                dve.wait_ge(roped, 5)
                dve.wait_ge(q_zeroed, Q_ZEROED["idx"])
                for h in range(8):
                    for odd in range(2):
                        at = 8 * odd + h
                        dve.tensor_copy(qmem[64 * odd:64 * odd + 64, at:at + 3 * 80 + 1:80],
                                        a_tiles[h // 2][64 * (h % 2):64 * (h % 2) + 64, SEQ + odd:T:2]).then_inc(q_placed, 1)
                dve.wait_ge(iw_ready, 1)
                dve.scalar_tensor_tensor(iws[:, :], ps[0:64, 5, 0:8], IDX_SCALE, selm, ALU.mult, ALU.mult)\
                   .then_inc(iw_done, 1)
                dve.wait_ge(iw_done, 2)
                k = 0
                for blk in range(1, NBLK):
                    sc = a_sc[:, SC0[blk]:SC0[blk] + (blk + 1) * P]
                    for h in range(8):
                        dve.wait_ge(ix_relu, k + 1)
                        r, w = tg[:, k % 2, 0:(blk + 1) * P], iwt[:, blk, h:h + 1]
                        if h == 0:
                            dve.tensor_scalar(sc, r, w, None, ALU.mult).then_inc(ix_added, 1)
                        else:
                            dve.wait_ge(ix_added, k)
                            dve.scalar_tensor_tensor(sc, r, w, sc, ALU.mult, ALU.add).then_inc(ix_added, 1)
                        k += 1
                    dve.wait_ge(ix_added, k)
                    own = a_sc[:, SC0[blk] + blk * P:SC0[blk] + (blk + 1) * P]
                    chain(dve.tensor_tensor(own, own, causal[:, :], ALU.add))
                dve.wait_ge(six_sum, 1)
                dve.tensor_copy(scs[0:8, 0:PAST], psf[0:8, 2048:2048 + PAST]).then_inc(six_done, 1)
                dve.tensor_tensor_reduce(tk[0:8, 1, 0:8], ps[0:8, 6, 0:8], ident[0:8, 0:8], 1.0, 0.0, ALU.mult, ALU.add,
                                         scs[0:8, PAST:PAST + 1]).then_inc(six_done, 1)
                dve.wait_ge(six_done, 2)
                dve.tensor_copy(tk[0:8, 1, 8:9], scs[0:8, PAST:PAST + 1]).then_inc(six_done, 1)
                dve.wait_ge(six_done, 3)

            def row_maximum(k):
                kind = ROW_KIND[k]
                rows, cols, at = nrows(kind), row_cols(kind), 1536 if kind == "mem" else 0
                if kind == "mem":
                    dve.wait_ge(r_used, max(it["r"] for it in items if (it["kind"], it["what"], it["layer"])
                                            == ("mem", "key", ROW_LAYER[k])) + 1)
                else:
                    dve.wait_ge(row_ready, k // 2 + 1)
                chain(dve.reduce_max(rstat[0:rows, k % 2, 0:1], psf[0:rows, at:at + cols], AX_X))
                settle()
                dve.tensor_scalar(rstat[0:rows, k % 2, 1:2], rstat[0:rows, k % 2, 0:1], -SCALE, None, ALU.mult)\
                   .then_inc(row_max, 1)

            def row_normalise(k):
                rows, cols = nrows(ROW_KIND[k]), row_cols(ROW_KIND[k])
                dve.wait_ge(row_exp, k + 1)
                chain(dve.reciprocal(rstat[0:rows, k % 2, 3:4], rstat[0:rows, k % 2, 2:3]))
                settle()
                p = rowp[k % 2][0:rows, 0:cols]
                dve.tensor_scalar(p, p, rstat[0:rows, k % 2, 3:4], None, ALU.mult).then_inc(row_norm, 1)

            def outputs_rest(k):
                M = mixers[ROW_LAYER[k]]
                for kt in range(M["out_kt"]):
                    dve.wait_ge(ot_head, M["ot0"] + kt + 1)
                    dve.tensor_tensor(actl[:, kt, 0:SEQ], ot[:, kt, 0:SEQ], acth[:, kt, 0:SEQ].bitcast(F32), ALU.subtract)\
                       .then_inc(ot_rest, 1)

            def row_copy_out(k):
                nh, o = nrows(ROW_KIND[k]) // NSAMP, OUT_AT[k % 2]
                dve.wait_ge(r_used, LAST_VALUES[k] + 1)
                dve.tensor_copy(rowo[o:o + nh, 1024:2048], psf[o:o + nh, 1024:2048]).then_inc(rowv_copied[k % 2], 1)

            def row_store(k):
                kind, nh, M = ROW_KIND[k], nrows(ROW_KIND[k]) // NSAMP, mixers[ROW_LAYER[k]]
                dve.wait_ge(rowo_ready, k + 1)
                if kind != "mem":
                    dve.wait_ge(new_copied, k // 2 + 1)
                for t, (ha, hb) in enumerate(PAIRS_A if kind == "a" else [(0, 1), (2, 3)]):
                    bank = 6 + t // 3 if kind == "a" else (4 if kind == "mem" else 6) + t
                    to = t if kind != "mem" else (6 if M["layer"] == 0 else 2) + t
                    for parts, h in ((slice(0, 64), ha), (slice(64, P), hb)):
                        out, old = ot[parts, to, SEQ:T], ps[parts, bank, h:h + (NSAMP - 1) * nh + 1:nh]
                        if kind == "mem":
                            c = dve.tensor_copy(out, old)
                        else:
                            new = rown[parts, bank - 6, h:h + (NSAMP - 1) * nh + 1:nh]
                            c = dve.tensor_tensor(out, old, new, ALU.add)
                c.then_inc(rowo_stored, 1)

            def sample_rows(layer):
                k = 2 * layer
                for b in (k, k + 1):
                    row_maximum(b)
                    row_normalise(b)
                outputs_rest(k)
                row_copy_out(k)
                for c in range(2):
                    split(mixers[layer]["out_chunk"] + c)
                row_copy_out(k + 1)
                row_store(k)
                row_store(k + 1)

            def tiles_out(M):
                nk = M["out_kt"]
                dve.wait_ge(ot_head, M["ot0"] + nk + 1)
                dve.tensor_tensor(actl[:, 0:nk, SEQ:T], ot[:, 0:nk, SEQ:T], acth[:, 0:nk, SEQ:T].bitcast(F32), ALU.subtract)\
                   .then_inc(ot_rest, 1)
                for m in range(KT):
                    done, count = out_done(M, m)
                    add_out(1.0, m, M["acc"], done, count)
                    if m == 0:
                        dve.wait_ge(ot_rest, M["ot0"] + nk + 1)
                    prepare(M["norm"] + 1, m)
                    if (m + 1) % out_tiles_per_chunk(M) == 0:
                        split(M["out_chunk"] + m // out_tiles_per_chunk(M) + 2)

            A, B = mixers
            memory_keys_values()
            ffn(0)
            dve.wait_ge(rope_loaded, 16 * 4)
            tiles_in(A, 0, 6)
            indexer()
            tiles_in(A, 6, 16)
            values_in(A)
            place_rows(A, (0, 1))
            attend(units[0], lambda k: search_steps(1))
            search_steps()
            sample_rows(0)
            tiles_out(A)
            ffn(1)
            ffn(2)
            tiles_in(B, 0, 14)
            values_in(B)
            place_rows(B, (2, 3))
            attend(units[1][:16])
            attend(units[1][16:])
            sample_rows(1)
            tiles_out(B)
            ffn(3)
            invert(6)
            dve.wait_ge(rstd_ready, 7)
            for m in range(KT):
                dve.scalar_tensor_tensor(y[:, m, :], y[:, m, :], gains[:, 6, m:m + 1], rstd[:, :], ALU.mult, ALU.mult)\
                   .then_inc(fin_ready, 1)

        @block.gpsimd
        def _(pool):
            def zero(k, buf):
                pool.memset(buf[:, :], 0.0).then_inc(q_zeroed, 1)

            def sum_squares(norm, first, last, i=None):
                for m in range(first, last):
                    more = 0 if i is None else 2 * i
                    pool.wait_ge(sq_ready, more + (KT * norm + m + 1))
                    if m == 0 and i is None:
                        pool.tensor_copy(ssum[:, :], tu[:, 0, :]).then_inc(ssum_done, 1)
                    else:
                        pool.wait_ge(ssum_done, more + (KT * norm + m))
                        pool.tensor_tensor(ssum[:, :], ssum[:, :], tu[:, m % 2, :], ALU.add).then_inc(ssum_done, 1)

            def ffn(f):
                g = FT * f
                for h in range(2):
                    with pool.Fori(0, HALF_TILES[h] // 2) as i:
                        for b in range(2):
                            pool.wait_ge(act_head, 2 * i + (g + b + 1))
                            at = bass.ds(2 * i + b, 1)
                            pool.tensor_tensor(actl[:, at, :].rearrange("p a t -> p (a t)"), tg[:, b, :],
                                               acth[:, at, :].rearrange("p a t -> p (a t)").bitcast(F32), ALU.subtract)\
                                .then_inc(act_rest, 1)
                    g += HALF_TILES[h]
                norm = [1, 3, 4, 6][f]
                sum_squares(norm, 0, 2)
                with pool.Fori(1, KT // 2) as i:
                    sum_squares(norm, 0, 2, i)

            def ropes(M):
                for j, t in enumerate(M["roped"]):
                    k = M["rope0"] + j
                    tile = M["tiles"][t]
                    pool.wait_ge(rot_ready, k + 1)
                    pool.tensor_tensor(tile, tile, cosf[:, :], ALU.mult).then_inc(cos_ready, 1)
                    pool.wait_ge(cos_ready, k + 1)
                    pool.wait_ge(sin_ready, k + 1)
                    pool.tensor_tensor(tile, tile, tg[:, k % 2, :], ALU.add).then_inc(roped, 1)

            def diagonals(us):
                for q in us:
                    pool.wait_ge(den_ready, q["u"] + 1)
                    pool.tensor_scalar(diag[:, q["u"] % 4, :], ident[:, :], stats[:, 3, q["u"] % 4:q["u"] % 4 + 1], None,
                                       ALU.mult).then_inc(p_ready, 1)

            A, B = mixers
            sum_squares(0, 0, KT)
            ffn(0)
            zero(1, qblk)
            pool.wait_ge(rms_ready, 2)
            zero("idx", qmem)
            pool.wait_ge(rope_loaded, 16 * 4)
            ropes(A)
            pool.wait_ge(r_used, 2)
            zero(0, qmem)
            diagonals(units[0])
            sum_squares(2, 0, KT)
            ffn(1)
            ffn(2)
            pool.wait_ge(rms_ready, 5)
            zero(3, qblk)
            zero(2, qmem)
            ropes(B)
            diagonals(units[1])
            sum_squares(5, 0, KT)
            ffn(3)


def kernel(x_prompt, x_sample, cache_kv_a, cache_kidx_a, state_kv_b1, state_kv_b2, state_kv_b3, cache_mem_kv,
           page_table, mem_prompt, ffn_norm, w_ffn_in, w_ffn_out, mix_norm, mem_norm, w_mem_kv, w_in_a, w_out_a,
           w_in_b, w_out_b, final_norm):
    import numpy as np
    from concourse import bacc
    from concourse.bass_utils import run_bass_kernel_spmd

    f32 = np.float32
    a = {}

    def feature_major(x):
        return np.ascontiguousarray(np.asarray(x).T.reshape(KT, P, -1).transpose(1, 0, 2))

    def chunks(w, cols, k_tiles, width):
        w = np.concatenate([np.asarray(w), np.zeros((w.shape[0], 1), f32)], axis=1)[:, cols]
        w = w.reshape(k_tiles, P, -1, width * P).transpose(2, 1, 0, 3)
        return np.ascontiguousarray(w.reshape(w.shape[0], P, -1))

    xs = np.concatenate([np.asarray(x_prompt)[0], np.asarray(x_sample)[:, 0]], axis=0)
    a["x"] = feature_major(xs)
    a["mem_x"] = feature_major(np.asarray(mem_prompt)[0])
    norms = [ffn_norm[0, 0], mix_norm[0], ffn_norm[0, 1], ffn_norm[1, 0], mix_norm[1], ffn_norm[1, 1], final_norm,
             mem_norm[0], mem_norm[1]]
    a["gains"] = np.ascontiguousarray(np.stack([np.asarray(g).reshape(KT, P) for g in norms]).transpose(2, 0, 1))
    w = np.asarray(w_ffn_in).reshape(NFFN, KT, P, 2, FT, P)
    a["w_ffn_in"] = np.ascontiguousarray(w.transpose(0, 4, 2, 1, 3, 5).reshape(NFFN * FT, P, CH))
    w = np.asarray(w_ffn_out).reshape(NFFN, FT, P, KT, P).transpose(0, 3, 2, 1, 4)
    w = w.reshape(NFFN * KT, P, FT, P)
    a["w_ffn_out0"] = np.ascontiguousarray(w[:, :, :HALF_TILES[0]]).reshape(NFFN * KT, P, -1)
    a["w_ffn_out1"] = np.ascontiguousarray(w[:, :, HALF_TILES[0]:]).reshape(NFFN * KT, P, -1)
    half = 4 * HD
    a["w_mem"] = np.concatenate([chunks(np.asarray(w_mem_kv)[i], np.arange(2 * half), KT, 2) for i in range(2)])

    def head(base, h):
        return base + h * HD + np.arange(HD)
    q0, k0, v0, iq0, ik0, iw0, mq0 = 0, 768, 1024, 1280, 1792, 1856, 1864
    cols = [iq0 + np.arange(512), ik0 + np.arange(HD), ik0 + np.arange(HD), iw0 + np.arange(8), np.full(P - 8, -1)]
    cols += [np.concatenate([head(q0, x), head(q0, z)]) for x, z in PAIRS_A]
    cols += [k0 + np.arange(half), mq0 + np.arange(half), v0 + np.arange(half)]
    a["w_in_a"] = chunks(np.asarray(w_in_a)[0], np.concatenate(cols), KT, 2)
    group = lambda g, part: (3 * g + part) * half + np.arange(half)
    cols = [group(g, part) for part in (0, 1) for g in range(3)] + [9 * half + np.arange(half)]
    cols += [group(g, 2) for g in range(3)]
    a["w_in_b"] = chunks(np.asarray(w_in_b)[0], np.concatenate(cols), KT, 2)
    order = np.concatenate([np.concatenate([head(0, x), head(0, z)]) for x, z in PAIRS_A] + [768 + np.arange(half)])
    a["w_out_a"] = chunks(np.asarray(w_out_a)[0][order], np.arange(D), 8, 2)
    a["w_out_b"] = chunks(np.asarray(w_out_b)[0], np.arange(D), 4, 4)

    pool = np.asarray(cache_kv_a)[0]
    n_pool = pool.shape[0]
    a["kpool"] = np.ascontiguousarray(pool[:, :, 0].reshape(n_pool, PAGE, 2, P).transpose(0, 3, 2, 1)).reshape(n_pool, P, 256)
    a["vpool"] = np.ascontiguousarray(pool[:, :, 1].reshape(n_pool, PAGE, 256))
    a["kidx"] = np.ascontiguousarray(np.asarray(cache_kidx_a)[0].transpose(0, 2, 1))
    a["pages"] = np.asarray(page_table).reshape(1, -1).astype(np.int32)

    def keys(c):
        b, n = c.shape[:2]
        return c.reshape(b, n, 2, P).transpose(0, 3, 2, 1)

    def by_items(c, per):
        return np.ascontiguousarray(c.reshape(NSAMP // per, per, P, -1).transpose(0, 2, 1, 3)).reshape(NSAMP // per, P, -1)

    mem = np.asarray(cache_mem_kv)
    per = ITEMS["mem"][0]
    a["mem_key"] = np.stack([by_items(keys(mem[i, :, :, 0]), per) for i in range(2)])
    a["mem_value"] = np.stack([by_items(mem[i, :, :, 1].reshape(NSAMP, 2, P, 256).transpose(0, 2, 1, 3), per)
                               for i in range(2)])
    states = [np.asarray(s)[0] for s in (state_kv_b1, state_kv_b2, state_kv_b3)]
    seen = [states[0], states[1][:, ::4], states[2][:, ::16]]
    per = ITEMS["b"][0]
    a["b_key"] = by_items(np.concatenate([keys(s[:, :, 0]).reshape(NSAMP, P, -1) for s in seen], axis=2), per)
    vals = [np.pad(s[:, :, 1].reshape(NSAMP, s.shape[1], 256), ((0, 0), (0, P - s.shape[1]), (0, 0))) for s in seen]
    a["b_value"] = by_items(np.stack(vals, axis=2), per)
    a["state0"] = np.ascontiguousarray(states[0][:, 1:]).reshape(NSAMP, 127, 512)
    a["state1"] = np.ascontiguousarray(states[1][:, 1:]).reshape(NSAMP, 511, 512)
    a["state2"] = np.ascontiguousarray(states[2]).reshape(NSAMP, 1024, 512)

    rot_half = HD // 8
    inv = (500000.0 ** (-np.arange(rot_half, dtype=np.float64) / rot_half)).astype(f32)
    pos = np.concatenate([np.arange(SEQ), np.full(NSAMP, PAST)]).astype(f32)
    ang = (pos[:, None] * inv[None, :]).astype(np.float64)
    cos, sin = np.ones((P, T), f32), np.zeros((P, T), f32)
    rot = np.zeros((P, P), f32)
    for h in (0, HD):
        for i in range(rot_half):
            cos[h + i] = cos[h + rot_half + i] = np.cos(ang[:, i])
            sin[h + i], sin[h + rot_half + i] = -np.sin(ang[:, i]), np.sin(ang[:, i])
            rot[h + rot_half + i, h + i] = rot[h + i, h + rot_half + i] = 1.0
    a["cos"], a["sin"], a["rot"], a["ident"] = cos, sin, rot, np.eye(P, dtype=f32)
    a["eps"] = np.full((P, 1), EPS, f32)
    a["causal"] = np.where(np.arange(P)[None, :] <= np.arange(P)[:, None], 0.0, NEG).astype(f32)
    small = np.zeros((P, 264), f32)
    for b in range(NSAMP):
        small[0:8, b * 8:b * 8 + 8] = np.eye(8)
        small[b * 8:b * 8 + 8, 64 + b] = 1.0
        small[b, 128 + b * 12:128 + (b + 1) * 12] = 1.0
    small[0:8, 224:232] = np.where(np.eye(8) > 0, 0.0, NEG)
    for r in range(32):
        for g in range(3):
            small[r, 232 + 8 * g:240 + 8 * g] = np.where(np.arange(8) == r // 4, 0.0, NEG)
    a["small"] = small
    masks = np.full((4, P, 768), NEG, f32)
    q, s = np.arange(P)[:, None], np.arange(SEQ)[None, :]
    for r in range(4):
        back = r + 4 * q - s
        masks[r, :, 0:SEQ][(back >= 0) & (back <= WINDOWS[0][0])] = 0.0
        back = q - np.arange(P)[None, :]
        masks[r, :, SEQ:SEQ + P][back >= 0] = 0.0
        masks[r, :, SEQ + P:][(back >= 0) & (back % 4 == 0)] = 0.0
    a["mask_b"] = masks

    out_shapes = {"y": (P, KT, T), "memk": (P, 2, 2, MEM), "memv": (P, 2, 2, MEM), "k_a": (P, 2, T),
                  "v_a": (P, NBLK, 256), "vs_a": (8, 256), "kidx": (64, T), "k_b": (P, 6, T),
                  "v_b": (P, 3, NBLK, 256), "vs_b": (8, 3, 256), "state0": (NSAMP, 127, 512),
                  "state1": (NSAMP, 511, 512), "state2": (NSAMP, 1024, 512)}
    nc = bacc.Bacc("TRN2", target_bir_lowering=False, num_devices=1)
    ins = {k: nc.dram_tensor(f"in_{k}", v.shape, mybir.dt.from_np(v.dtype), kind="ExternalInput").ap() for k, v in a.items()}
    outs = {k: nc.dram_tensor(f"out_{k}", s, F32, kind="ExternalOutput").ap() for k, s in out_shapes.items()}
    build(nc, ins, outs)
    r = run_bass_kernel_spmd(nc, [{f"in_{k}": v for k, v in a.items()}], core_ids=[0]).results[0]
    r = {k: np.asarray(r[f"out_{k}"]) for k in out_shapes}

    yt = r["y"].transpose(2, 1, 0).reshape(T, D)
    y_prompt, y_sample = yt[None, :SEQ], yt[SEQ:, None]
    mk = r["memk"].transpose(1, 3, 2, 0).reshape(2, MEM, 4, HD)
    mv = r["memv"].transpose(1, 2, 0, 3).reshape(2, MEM, 4, HD)
    new_mem = np.stack([mk, mv], axis=2)[:, None]
    ka = r["k_a"].transpose(2, 1, 0).reshape(T, 4, HD)
    va = np.concatenate([r["v_a"].transpose(1, 0, 2).reshape(SEQ, 4, HD), r["vs_a"].reshape(8, 4, HD)])
    kv_a = np.stack([ka, va], axis=1)
    kidx = r["kidx"].T
    kb = r["k_b"].reshape(P, 3, 2, T).transpose(1, 3, 2, 0).reshape(3, T, 4, HD)
    vb = r["v_b"].transpose(1, 2, 0, 3)
    vb = np.stack([vb[0].reshape(SEQ, 256)] + [vb[g].transpose(1, 0, 2).reshape(SEQ, 256) for g in (1, 2)])
    vb = np.concatenate([vb, r["vs_b"].transpose(1, 0, 2)], axis=1).reshape(3, T, 4, HD)
    kv_b = np.stack([kb, vb], axis=2)
    new_b_prompt = [kv_b[g, SEQ - min(w, SEQ):SEQ][None, None] for g, (w, _) in enumerate(WINDOWS)]
    new_b_sample = [np.concatenate([r[f"state{g}"].reshape(NSAMP, -1, 2, 4, HD), kv_b[g, SEQ:, None]], axis=1)[None]
                    for g in range(3)]
    return (y_prompt, y_sample, kv_a[None, None, :SEQ], kidx[None, None, :SEQ], *new_b_prompt, new_mem,
            kv_a[None, SEQ:, None], kidx[None, SEQ:, None], *new_b_sample)
```
